# Optimizing a Trainium2 kernel written in Bass

```python
import math
import jax
import jax.numpy as jnp
from jax import lax
import numpy as np

D_MODEL = 1024
BATCH = 1
SEQ = 256
DEPTH = 2
DEC_BATCH = 8
DEC_SEQ = 1
PAST_LEN = 2048
PAGE_SIZE = 128

GDN_HEADS = 4
GDN_DK = 128
GDN_DV = 128
GDN_CONV = 4
MLA_HEADS = 8
MLA_Q_LORA = 256
MLA_KV_LORA = 128
MLA_NOPE = 64
MLA_ROPE = 32
MLA_VDIM = 64
ROPE_BASE = 10000.0
ATTN_BLOCK = 128
ML_HEADS = 4
ML_DK = 64
ML_DV = 128
CHUNK = 64
D_FF = 2816
FFN_CONV = 3
NORM_EPS = 1e-6

GDN_QK = GDN_HEADS * GDN_DK
GDN_V = GDN_HEADS * GDN_DV
GDN_QKV = 2 * GDN_QK + GDN_V
MLA_QHEAD = MLA_NOPE + MLA_ROPE
MLA_V = MLA_HEADS * MLA_VDIM
MLA_SCALE = MLA_QHEAD ** -0.5
ML_QK = ML_HEADS * ML_DK
ML_V = ML_HEADS * ML_DV
ML_QKV = 2 * ML_QK + ML_V
IN_SIZES = (GDN_QKV, GDN_HEADS, GDN_HEADS, GDN_V, MLA_Q_LORA, MLA_KV_LORA, MLA_ROPE, ML_QKV, ML_HEADS, ML_HEADS, ML_V, 3 * D_MODEL)
IN_WIDTH = sum(IN_SIZES)

kernel_name = 'hybrid_gdn_mla_mlstm_convffn_step'

def rmsnorm(x, g):
    xf = x.astype(jnp.float32)
    y = xf * lax.rsqrt(jnp.mean(xf * xf, axis=-1, keepdims=True) + NORM_EPS)
    return (y * g.astype(jnp.float32)).astype(x.dtype)

def l2norm(x):
    xf = x.astype(jnp.float32)
    return xf * lax.rsqrt(jnp.sum(xf * xf, axis=-1, keepdims=True) + NORM_EPS)

def causal_dwconv(x, hist, w):
    width, length = w.shape[0], x.shape[1]
    xp = jnp.concatenate([hist.astype(x.dtype), x], axis=1)
    y = xp[:, 0:length] * w[0]
    for j in range(1, width):
        y = y + xp[:, j:j + length] * w[j]
    return y, xp[:, length:]

def rope(x, pos):
    half = x.shape[-1] // 2
    inv_freq = ROPE_BASE ** (-jnp.arange(half, dtype=jnp.float32) / half)
    ang = pos.astype(jnp.float32)[:, None] * inv_freq[None, :]
    bshape = (ang.shape[0],) + (1,) * (x.ndim - 3) + (half,)
    cos, sin = jnp.cos(ang).reshape(bshape), jnp.sin(ang).reshape(bshape)
    xf = x.astype(jnp.float32)
    x1, x2 = xf[..., :half], xf[..., half:]
    return jnp.concatenate([x1 * cos - x2 * sin, x1 * sin + x2 * cos], axis=-1).astype(x.dtype)

def to_chunks(a, chunk):
    b, t = a.shape[:2]
    return jnp.swapaxes(a.reshape((b, t // chunk, chunk) + a.shape[2:]), 2, 3)

def causal_masks(n):
    idx = jnp.arange(n)
    return idx[:, None] >= idx[None, :], idx[:, None] > idx[None, :]

def gated_delta_rule(q, k, v, beta, g, S0, chunk):
    b, t, h, dk = q.shape
    dv = v.shape[-1]
    q, k, v, beta, g = [to_chunks(a.astype(jnp.float32), chunk) for a in (q, k, v, beta, g)]
    incl, strict = causal_masks(chunk)
    G = jnp.cumsum(g, axis=-1)
    dec_incl = jnp.exp(jnp.where(incl, G[..., :, None] - G[..., None, :], -jnp.inf))
    A = beta[..., :, None] * jnp.einsum('bnhld,bnhmd->bnhlm', k, k) * jnp.where(strict, dec_incl, 0.0)
    IA = A + jnp.eye(chunk, dtype=jnp.float32)
    U = lax.linalg.triangular_solve(IA, beta[..., None] * v, left_side=True, lower=True, unit_diagonal=True)
    W = lax.linalg.triangular_solve(IA, (beta * jnp.exp(G))[..., None] * k, left_side=True, lower=True, unit_diagonal=True)
    QK = jnp.einsum('bnhld,bnhmd->bnhlm', q, k) * dec_incl
    q_dec = q * jnp.exp(G)[..., None]
    k_dec = k * jnp.exp(G[..., -1:] - G)[..., None]
    g_last = jnp.exp(G[..., -1])

    def step(S, xs):
        U_c, W_c, QK_c, qd_c, kd_c, gl_c = xs
        v_new = U_c - jnp.einsum('bhld,bhde->bhle', W_c, S)
        o = jnp.einsum('bhld,bhde->bhle', qd_c, S) + jnp.einsum('bhlm,bhme->bhle', QK_c, v_new)
        S = gl_c[..., None, None] * S + jnp.einsum('bhld,bhle->bhde', kd_c, v_new)
        return S, o

    xs = tuple(jnp.moveaxis(a, 1, 0) for a in (U, W, QK, q_dec, k_dec, g_last))
    S, o = lax.scan(step, S0.astype(jnp.float32), xs)
    o = jnp.transpose(o, (1, 0, 3, 2, 4)).reshape(b, t, h, dv)
    return o, S

def mlstm_chunked(q, k, v, i_pre, logf, C0, n0, m0, chunk):
    b, t, h, dk = q.shape
    dv = v.shape[-1]
    q, k, v, i_pre, logf = [to_chunks(a.astype(jnp.float32), chunk) for a in (q, k, v, i_pre, logf)]
    incl, _ = causal_masks(chunk)
    F = jnp.cumsum(logf, axis=-1)
    D = jnp.where(incl, F[..., :, None] - F[..., None, :] + i_pre[..., None, :], -jnp.inf)
    D_max = jnp.max(D, axis=-1)
    QK = jnp.einsum('bnhld,bnhmd->bnhlm', q, k)

    def step(carry, xs):
        C, n, m = carry
        q_c, k_c, v_c, F_c, D_c, Dm_c, QK_c = xs
        b_log = F_c + m[..., None]
        m_r = jnp.maximum(b_log, Dm_c)
        inter = jnp.exp(b_log - m_r)
        P = jnp.exp(D_c - m_r[..., None]) * QK_c
        num = inter[..., None] * jnp.einsum('bhld,bhde->bhle', q_c, C) + jnp.einsum('bhlm,bhme->bhle', P, v_c)
        den = inter * jnp.einsum('bhld,bhd->bhl', q_c, n) + jnp.sum(P, axis=-1)
        h_t = num / jnp.maximum(jnp.abs(den), jnp.exp(-m_r))[..., None]
        m_new = m_r[..., -1]
        w_key = jnp.exp(D_c[..., -1, :] - m_new[..., None])
        carry_decay = jnp.exp(b_log[..., -1] - m_new)
        C = carry_decay[..., None, None] * C + jnp.einsum('bhl,bhld,bhle->bhde', w_key, k_c, v_c)
        n = carry_decay[..., None] * n + jnp.einsum('bhl,bhld->bhd', w_key, k_c)
        return (C, n, m_new), h_t

    xs = tuple(jnp.moveaxis(a, 1, 0) for a in (q, k, v, F, D, D_max, QK))
    init = (C0.astype(jnp.float32), n0.astype(jnp.float32), m0.astype(jnp.float32))
    (C, n, m), hs = lax.scan(step, init, xs)
    hs = jnp.transpose(hs, (1, 0, 3, 2, 4)).reshape(b, t, h, dv)
    return hs, C, n, m

def mla_prompt_attention(q_nope, q_rope, c_kv, k_rope, w_uk, w_uv):
    bsz, length = c_kv.shape[:2]
    k_nope = jnp.einsum('bsc,chd->bshd', c_kv, w_uk.reshape(MLA_KV_LORA, MLA_HEADS, MLA_NOPE))
    v = jnp.einsum('bsc,chd->bshd', c_kv, w_uv.reshape(MLA_KV_LORA, MLA_HEADS, MLA_VDIM))
    n_blk = length // ATTN_BLOCK

    def blocks(a):
        return jnp.swapaxes(a.reshape((bsz, n_blk, ATTN_BLOCK) + a.shape[2:]), 0, 1)

    kpos = jnp.arange(length)

    def attend_block(args):
        qn, qr, start = args
        s = jnp.einsum('bqhd,bkhd->bhqk', qn, k_nope) + jnp.einsum('bqhr,bkr->bhqk', qr, k_rope)
        qpos = start + jnp.arange(ATTN_BLOCK)
        s = jnp.where(kpos[None, :] <= qpos[:, None], s.astype(jnp.float32) * MLA_SCALE, -jnp.inf)
        p = jax.nn.softmax(s, axis=-1).astype(v.dtype)
        return jnp.einsum('bhqk,bkhd->bqhd', p, v)

    out = lax.map(attend_block, (blocks(q_nope), blocks(q_rope), jnp.arange(n_blk) * ATTN_BLOCK))
    return jnp.swapaxes(out, 0, 1).reshape(bsz, length, MLA_HEADS, MLA_VDIM)

def mla_sample_attention(q_nope, q_rope, c_kv, k_rope, w_uk, w_uv, lat_past, kr_past):
    length = c_kv.shape[1]
    past = lat_past.shape[1]
    q_lat = jnp.einsum('bqhd,chd->bqhc', q_nope, w_uk.reshape(MLA_KV_LORA, MLA_HEADS, MLA_NOPE))
    s_past = jnp.einsum('bqhc,bkc->bhqk', q_lat, lat_past) + jnp.einsum('bqhr,bkr->bhqk', q_rope, kr_past)
    s_new = jnp.einsum('bqhc,bkc->bhqk', q_lat, c_kv) + jnp.einsum('bqhr,bkr->bhqk', q_rope, k_rope)
    incl, _ = causal_masks(length)
    s = jnp.concatenate([s_past.astype(jnp.float32) * MLA_SCALE,
                         jnp.where(incl, s_new.astype(jnp.float32) * MLA_SCALE, -jnp.inf)], axis=-1)
    p = jax.nn.softmax(s, axis=-1).astype(lat_past.dtype)
    ctx = (jnp.einsum('bhqk,bkc->bqhc', p[..., :past], lat_past)
           + jnp.einsum('bhqk,bkc->bqhc', p[..., past:], c_kv.astype(lat_past.dtype)))
    return jnp.einsum('bqhc,chd->bqhd', ctx, w_uv.reshape(MLA_KV_LORA, MLA_HEADS, MLA_VDIM))

def mixer(h, pos, gdn_conv0, gdn_S0, ml_C0, ml_n0, ml_m0, attend, chunk,
          w_in, gdn_conv_w, gdn_A_log, gdn_dt_bias, gdn_norm_g,
          mla_q_norm_g, mla_w_uq, mla_kv_norm_g, mla_w_uk, mla_w_uv,
          ml_b_i, ml_b_f, ml_norm_g, w_branch_a, w_branch_b, w_branch_c, w_out):
    bsz, length, _ = h.shape
    f32 = jnp.float32
    z = h @ w_in
    (a_qkv, a_beta, a_alpha, a_z, b_cq, b_ckv, b_kr,
     c_qkv, c_i, c_f, c_o, gates) = jnp.split(z, np.cumsum(IN_SIZES)[:-1].tolist(), axis=-1)
    a_qkv, gdn_conv = causal_dwconv(a_qkv, gdn_conv0, gdn_conv_w)
    a_qkv = jax.nn.silu(a_qkv)
    aq, ak, av = jnp.split(a_qkv, [GDN_QK, 2 * GDN_QK], axis=-1)
    aq = l2norm(aq.reshape(bsz, length, GDN_HEADS, GDN_DK)) * (GDN_DK ** -0.5)
    ak = l2norm(ak.reshape(bsz, length, GDN_HEADS, GDN_DK))
    av = av.reshape(bsz, length, GDN_HEADS, GDN_DV)
    beta = jax.nn.sigmoid(a_beta.astype(f32))
    g = -jnp.exp(gdn_A_log.astype(f32)) * jax.nn.softplus(a_alpha.astype(f32) + gdn_dt_bias.astype(f32))
    o_a, gdn_S = gated_delta_rule(aq, ak, av, beta, g, gdn_S0, chunk)
    o_a = rmsnorm(o_a, gdn_norm_g) * jax.nn.silu(a_z.astype(f32)).reshape(bsz, length, GDN_HEADS, GDN_DV)
    o_a = o_a.reshape(bsz, length, GDN_V).astype(h.dtype)
    q = (rmsnorm(b_cq, mla_q_norm_g) @ mla_w_uq).reshape(bsz, length, MLA_HEADS, MLA_QHEAD)
    q_nope, q_rope = q[..., :MLA_NOPE], rope(q[..., MLA_NOPE:], pos)
    c_kv = rmsnorm(b_ckv, mla_kv_norm_g)
    k_rope = rope(b_kr, pos)
    o_b = attend(q_nope, q_rope, c_kv, k_rope, mla_w_uk, mla_w_uv).reshape(bsz, length, MLA_V).astype(h.dtype)
    cq, ck, cv = jnp.split(c_qkv, [ML_QK, 2 * ML_QK], axis=-1)
    cq = cq.reshape(bsz, length, ML_HEADS, ML_DK)
    ck = ck.reshape(bsz, length, ML_HEADS, ML_DK) * (ML_DK ** -0.5)
    cv = cv.reshape(bsz, length, ML_HEADS, ML_DV)
    i_pre = c_i.astype(f32) + ml_b_i.astype(f32)
    logf = jax.nn.log_sigmoid(c_f.astype(f32) + ml_b_f.astype(f32))
    h_c, ml_C, ml_n, ml_m = mlstm_chunked(cq, ck, cv, i_pre, logf, ml_C0, ml_n0, ml_m0, chunk)
    o_gate = jax.nn.sigmoid(c_o.astype(f32)).reshape(bsz, length, ML_HEADS, ML_DV)
    o_c = rmsnorm(o_gate * h_c, ml_norm_g).reshape(bsz, length, ML_V).astype(h.dtype)
    g_a, g_b, g_c = jnp.split(jax.nn.sigmoid(gates), 3, axis=-1)
    merged = g_a * (o_a @ w_branch_a) + g_b * (o_b @ w_branch_b) + g_c * (o_c @ w_branch_c)
    return merged @ w_out, (c_kv, k_rope, gdn_conv, gdn_S, ml_C, ml_n, ml_m)

def conv_ffn(h, conv0, w_up, conv_w, conv_b, w_down):
    u, gt = jnp.split(h @ w_up, 2, axis=-1)
    gt_c, new_buf = causal_dwconv(gt, conv0, conv_w)
    return (jax.nn.silu(gt_c + conv_b) * u) @ w_down, new_buf

def setup_inputs(seed: int = 0) -> dict:
    key = jax.random.key(seed)
    keys = jax.random.split(key, 40)
    f32 = jnp.float32
    n_pages = PAST_LEN // PAGE_SIZE
    n_pool = (DEC_BATCH * n_pages * 5) // 4

    def nrm(i, shape, scale=1.0):
        return jax.random.normal(keys[i], shape, f32) * scale

    def gain(i, shape):
        return 1.0 + nrm(i, shape, 0.02)

    page_table = jax.random.permutation(keys[0], n_pool)[:DEC_BATCH * n_pages].reshape(DEC_BATCH, n_pages).astype(jnp.int32)
    dt = jnp.exp(jax.random.uniform(keys[1], (DEPTH, GDN_HEADS), f32, math.log(1e-3), math.log(1e-1)))
    return {
        'x_prompt': nrm(2, (BATCH, SEQ, D_MODEL)),
        'x_sample': nrm(3, (DEC_BATCH, DEC_SEQ, D_MODEL)),
        'cache_kv_latent': nrm(4, (DEPTH, n_pool, PAGE_SIZE, MLA_KV_LORA)),
        'cache_k_rope': nrm(5, (DEPTH, n_pool, PAGE_SIZE, MLA_ROPE)),
        'state_gdn_conv': nrm(6, (DEPTH, DEC_BATCH, GDN_CONV - 1, GDN_QKV)),
        'state_gdn_S': nrm(7, (DEPTH, DEC_BATCH, GDN_HEADS, GDN_DK, GDN_DV), GDN_DK ** -0.5),
        'state_mlstm_C': nrm(8, (DEPTH, DEC_BATCH, ML_HEADS, ML_DK, ML_DV)),
        'state_mlstm_n': nrm(9, (DEPTH, DEC_BATCH, ML_HEADS, ML_DK)),
        'state_mlstm_m': nrm(10, (DEPTH, DEC_BATCH, ML_HEADS)),
        'state_ffn_conv': nrm(11, (DEPTH, DEC_BATCH, FFN_CONV - 1, D_FF)),
        'page_table': page_table,
        'norm1_g': gain(12, (DEPTH, D_MODEL)),
        'w_in': nrm(13, (DEPTH, D_MODEL, IN_WIDTH), D_MODEL ** -0.5),
        'gdn_conv_w': nrm(14, (DEPTH, GDN_CONV, GDN_QKV), GDN_CONV ** -0.5),
        'gdn_A_log': jnp.log(jax.random.uniform(keys[15], (DEPTH, GDN_HEADS), f32, 1.0, 16.0)),
        'gdn_dt_bias': dt + jnp.log(-jnp.expm1(-dt)),
        'gdn_norm_g': gain(16, (DEPTH, GDN_DV)),
        'mla_q_norm_g': gain(17, (DEPTH, MLA_Q_LORA)),
        'mla_w_uq': nrm(18, (DEPTH, MLA_Q_LORA, MLA_HEADS * MLA_QHEAD), MLA_Q_LORA ** -0.5),
        'mla_kv_norm_g': gain(19, (DEPTH, MLA_KV_LORA)),
        'mla_w_uk': nrm(20, (DEPTH, MLA_KV_LORA, MLA_HEADS * MLA_NOPE), MLA_KV_LORA ** -0.5),
        'mla_w_uv': nrm(21, (DEPTH, MLA_KV_LORA, MLA_HEADS * MLA_VDIM), MLA_KV_LORA ** -0.5),
        'ml_b_i': nrm(22, (DEPTH, ML_HEADS), 0.1),
        'ml_b_f': jnp.linspace(3.0, 6.0, ML_HEADS, dtype=f32)[None, :] + nrm(23, (DEPTH, ML_HEADS), 0.1),
        'ml_norm_g': gain(24, (DEPTH, ML_DV)),
        'w_branch_a': nrm(25, (DEPTH, GDN_V, D_MODEL), GDN_V ** -0.5),
        'w_branch_b': nrm(26, (DEPTH, MLA_V, D_MODEL), MLA_V ** -0.5),
        'w_branch_c': nrm(27, (DEPTH, ML_V, D_MODEL), ML_V ** -0.5),
        'w_out': nrm(28, (DEPTH, D_MODEL, D_MODEL), D_MODEL ** -0.5),
        'norm2_g': gain(29, (DEPTH, D_MODEL)),
        'ffn_w_up': nrm(30, (DEPTH, D_MODEL, 2 * D_FF), D_MODEL ** -0.5),
        'ffn_conv_w': nrm(31, (DEPTH, FFN_CONV, D_FF), FFN_CONV ** -0.5),
        'ffn_conv_b': nrm(32, (DEPTH, D_FF), 0.02),
        'ffn_w_down': nrm(33, (DEPTH, D_FF, D_MODEL), D_FF ** -0.5),
        'final_norm_g': gain(34, (D_MODEL,)),
    }

def reference(x_prompt, x_sample, cache_kv_latent, cache_k_rope, state_gdn_conv, state_gdn_S,
              state_mlstm_C, state_mlstm_n, state_mlstm_m, state_ffn_conv, page_table,
              norm1_g, w_in, gdn_conv_w, gdn_A_log, gdn_dt_bias, gdn_norm_g,
              mla_q_norm_g, mla_w_uq, mla_kv_norm_g, mla_w_uk, mla_w_uv,
              ml_b_i, ml_b_f, ml_norm_g, w_branch_a, w_branch_b, w_branch_c, w_out,
              norm2_g, ffn_w_up, ffn_conv_w, ffn_conv_b, ffn_w_down, final_norm_g):
    f32 = jnp.float32
    bp, seq = x_prompt.shape[:2]
    bs, dec = x_sample.shape[:2]
    past_len = page_table.shape[1] * PAGE_SIZE
    pos_p = jnp.arange(seq)
    pos_s = past_len + jnp.arange(dec)
    xp, xs = x_prompt, x_sample
    out_p = [[] for _ in range(8)]
    out_s = [[] for _ in range(8)]
    for l in range(DEPTH):
        lp = (w_in[l], gdn_conv_w[l], gdn_A_log[l], gdn_dt_bias[l], gdn_norm_g[l],
              mla_q_norm_g[l], mla_w_uq[l], mla_kv_norm_g[l], mla_w_uk[l], mla_w_uv[l],
              ml_b_i[l], ml_b_f[l], ml_norm_g[l], w_branch_a[l], w_branch_b[l], w_branch_c[l], w_out[l])
        m_out, st = mixer(rmsnorm(xp, norm1_g[l]), pos_p,
                          jnp.zeros((bp, GDN_CONV - 1, GDN_QKV), xp.dtype),
                          jnp.zeros((bp, GDN_HEADS, GDN_DK, GDN_DV), f32),
                          jnp.zeros((bp, ML_HEADS, ML_DK, ML_DV), f32),
                          jnp.zeros((bp, ML_HEADS, ML_DK), f32),
                          jnp.zeros((bp, ML_HEADS), f32),
                          mla_prompt_attention, CHUNK, *lp)
        xp = xp + m_out
        f_out, f_buf = conv_ffn(rmsnorm(xp, norm2_g[l]), jnp.zeros((bp, FFN_CONV - 1, D_FF), xp.dtype),
                                ffn_w_up[l], ffn_conv_w[l], ffn_conv_b[l], ffn_w_down[l])
        xp = xp + f_out
        for lst, a in zip(out_p, st + (f_buf,)):
            lst.append(a)
        lat_past = cache_kv_latent[l, page_table].reshape(bs, past_len, MLA_KV_LORA)
        kr_past = cache_k_rope[l, page_table].reshape(bs, past_len, MLA_ROPE)

        def attend_sample(qn, qr, ckv, kr, wuk, wuv, lat_past=lat_past, kr_past=kr_past):
            return mla_sample_attention(qn, qr, ckv, kr, wuk, wuv, lat_past, kr_past)

        m_out, st = mixer(rmsnorm(xs, norm1_g[l]), pos_s,
                          state_gdn_conv[l], state_gdn_S[l], state_mlstm_C[l], state_mlstm_n[l], state_mlstm_m[l],
                          attend_sample, dec, *lp)
        xs = xs + m_out
        f_out, f_buf = conv_ffn(rmsnorm(xs, norm2_g[l]), state_ffn_conv[l],
                                ffn_w_up[l], ffn_conv_w[l], ffn_conv_b[l], ffn_w_down[l])
        xs = xs + f_out
        for lst, a in zip(out_s, st + (f_buf,)):
            lst.append(a)
    y_prompt = rmsnorm(xp, final_norm_g)
    y_sample = rmsnorm(xs, final_norm_g)
    p_ckv, p_kr, p_gconv, p_gS, p_C, p_n, p_m, p_fconv = [jnp.stack(a) for a in out_p]
    s_ckv, s_kr, s_gconv, s_gS, s_C, s_n, s_m, s_fconv = [jnp.stack(a) for a in out_s]
    return (y_prompt, y_sample, p_ckv, p_kr, p_gconv, p_gS, p_C, p_n, p_m, p_fconv,
            s_ckv, s_kr, s_gconv, s_gS, s_C, s_n, s_m, s_fconv)


_drawn_inputs = setup_inputs


def setup_inputs(seed=0):
    import zlib

    import numpy as np

    out = dict(_drawn_inputs(seed))
    spreads = {}
    factors = {'cache_k_rope': 4.525,
     'gdn_norm_g': 6.115,
     'mla_q_norm_g': 8.0,
     'mla_kv_norm_g': 2.916,
     'ml_norm_g': 3.296,
     'ffn_conv_b': 3.876,
     'final_norm_g': 7.85,
     'norm2_g': 2.715}
    for name, (base, spread) in spreads.items():
        noise = np.random.default_rng([zlib.crc32(name.encode()), seed]).standard_normal(out[name].shape)
        drawn = base * np.exp(spread * noise) if base else spread * noise
        out[name] = jnp.asarray(drawn.astype(out[name].dtype))
    for name, factor in factors.items():
        out[name] = (out[name] * factor).astype(out[name].dtype)
    return out
```

```python
from contextlib import ExitStack

import numpy as np
import concourse.bass as bass
from concourse import mybir

F32 = mybir.dt.float32
I32 = mybir.dt.int32
U32 = mybir.dt.uint32
ALU = mybir.AluOpType
ACT = mybir.ActivationFunctionType
AX_X = mybir.AxisListType.X

P = 128
D, KT = 1024, 8
L = 2
TP, NB = 256, 8
TT = TP + NB
NH = 4
MH = 8
NCH = 2
FFC = 22
PAST, PAGE = 2048, 128
NPAGE = PAST // PAGE
NPOOL = NB * NPAGE * 5 // 4
NR = 16
EPS = 1e-6
SCALE = float(96) ** -0.5
LEVELS = 7
NS = NH * NB

SLOTS = 11
N_IN = 33
UNITS = N_IN + 24 + 12 + 8 + 2 * FFC + FFC
assert UNITS % SLOTS == 0

C_ID, C_ONE, C_INC, C_LVL = 0, 128, 256, 384
C_CAUS = C_LVL + LEVELS * 128
C_ROPE = C_CAUS + 384
C_PM = C_ROPE + TT
N_CONST = C_PM + 1
Q_N1, Q_N2, Q_CW = 0, 8, 16
Q_GN, Q_QN, Q_KN, Q_MN = 64, 65, 67, 68
Q_FW, Q_FB, Q_NF = 69, 135, 157
Q_ROW = 165
N_PAR = 169


def schedule():
    s = []

    def add(name, n=1, reader="A"):
        s.extend((name, i, reader) for i in range(n))

    fills = [("pm", i, "A") for i in range(12)] + [("pa", 0, "A"), ("pa", 1, "V"), ("pa", 2, "A"), ("pa", 3, "A")]

    def fill(n):
        for _ in range(n):
            s.append(fills.pop(0))

    add("n1"); add("pS", 1, "V"); add("pq", 12)
    add("pz", 4, "V")
    add("l2", 8)
    add("rowT", 1, "V")
    for h in range(NH):
        s += [("bcB", h, "V"), ("bcG", h, "V"), ("bcE", h, "V")]
    fill(2)
    add("kT", 2); add("vT", 2, "V")
    add("aq", 8, "V")
    for j in range(LEVELS):
        s += [("Y", 2 * j, "A"), ("Y", 2 * j + 1, "A")]
        if j < LEVELS - 1:
            s += [("T", 2 * j, "V"), ("T", 2 * j + 1, "V")]
        s += [("TT", 2 * j, "V"), ("TT", 2 * j + 1, "V")]
        fill(1)
    add("vn0"); add("o0"); add("s1"); fill(1)
    add("ks", 1, "V"); fill(1); add("vn1"); add("o1"); add("s2", 1, "V")
    add("sk", 1, "V"); add("qk", 1, "V"); fill(2); add("kvT"); add("out", 8, "V")
    add("na", 4); fill(3)
    assert not fills
    for h in range(NH):
        s += [("bcM", h, "V"), ("bcI", h, "V"), ("bcR", h, "A")]
    add("bcW", 1, "V")
    add("mkT", 2); add("mvT", 2); add("mqk", 2, "V")
    add("md0"); add("mn0", 1, "V"); add("mc1", 2)
    add("md1"); add("mn1", 1, "V"); add("mc2", 2, "V")
    add("mq", 1, "V"); add("mqn", 1, "V"); add("mkvT"); add("mout", 8, "V")
    add("nc", 4)
    add("nk"); add("nq")
    add("uq", 8, "V"); add("uk", 4); add("uv", 2); add("ql")
    add("sc", 8, "V"); add("ptT", 6); add("pv", 4)
    add("sn", 1, "V")
    for b in range(NB + 1):
        if b < NB:
            s.append(("krT", b, "A"))
            s += [("ltr", 4 * b + q, "AV"[q % 2]) for q in range(4)]
            s.append(("ss", b, "V"))
        if b > 0:
            s.append(("cs", b - 1, "V"))
        if b < NB:
            s += [("mxT", b, "V"), ("mxB", b, "V")]
    add("ov")
    for n in range(8):
        s += [("pg", 3 * n + i, "A") for i in range(3)] + [("pb", 3 * n + i, "V") for i in range(3)]
    add("pw", 8, "V"); add("n2")
    for j in range(FFC):
        s += [("fg", j, "A"), ("fu", j, "V")]
    add("fd", 8, "V")
    return s


SCHED = schedule()
WHERE = {(n, i): k for k, (n, i, _) in enumerate(SCHED)}
READS = {"A": [e[:2] for e in SCHED if e[2] == "A"], "V": [e[:2] for e in SCHED if e[2] == "V"]}
RANK = {e: (r, k) for r in READS for k, e in enumerate(READS[r])}


SIGNALS = dict(
    beta_tanh=1, c_decayed=1, c_loaded=16, conv=12, conv_state=1, conv_tanh=12, decay_exp=1, decay_in=4,
    decay_masked=1, ffn_conv=22, ffn_sconv=1, ffn_stanh=1, ffn_tail=22, ffn_tanh=22, ffn_zeros=1, fh_loaded=16,
    hidden=1, hidden_norm=2, hist_loaded=16, key_copied=1, lat_in0=128, lat_in1=128, latent_norm=1, latent_out=1,
    latent_squares=1, level_a=14, m_loaded=16, mdecay_exp=1, mdecay_in=4, mdecay_masked=1, merged=8, mla_loaded=16,
    msample_kv=1, msample_prods=1, mv_diag=8, n_loaded=16, n_new=1, neg_max=1, new_prods=1, next_rows=1, oa_done=1,
    oa_squares=1, oc_done=1, oc_raw=1, oc_squares=1, ones_column=1, page_exp=8, page_max=8, page_sub=8,
    page_sums=8, par_loaded=16, probs=1, probs_raw=1, qk_squares=1, qk_unit=1, query_blocks=1, row_e=1, row_ea=1,
    row_ln=1, row_m=1, row_m0=1, row_u=1, row_x=1, rows_act=1, rows_dve=1, s_decayed=1, s_loaded=16,
    sample_prods=1, sample_vnew=1, sconv=1, sconv_tanh=1, silu=13, squares=2, st_ckv=16, st_conv=16, st_ffn=16,
    st_kr=16, st_m=16, st_pc=16, st_ps=16, st_sc=128, st_sn=16, st_ss=128, v_diag=8, z_tanh=4,
)


class Region:

    def __init__(self, arena, at, end):
        self.arena, self.at, self.end = arena, at, end

    def take(self, n, p=P):
        a = self.at
        self.at += n
        assert self.at <= self.end, (self.at, self.end)
        return self.arena[0:p, a:a + n]

    def take3(self, k, n, p=P):
        return self.take(k * n, p).rearrange("p (k n) -> p k n", k=k)


ARENA = 52600


def build(nc, a):
    with ExitStack() as ctx:
        arena = ctx.enter_context(nc.sbuf_tensor("arena", [P, ARENA], F32))
        idx_raw = ctx.enter_context(nc.sbuf_tensor("idx_raw", [P, NB], I32))
        page_row = ctx.enter_context(nc.sbuf_tensor("page_row", [P, NB], U32))
        banks = ctx.enter_context(nc.psum_tensor("banks", [P, 8, 512], F32))

        fix = Region(arena, 0, ARENA)
        x = fix.take3(KT, TT)
        hn = fix.take3(KT, TT)
        ring = fix.take(SLOTS * 1024)
        const = fix.take(N_CONST)
        par = fix.take(N_PAR)
        oa = fix.take3(4, TT)
        ob_at = fix.at
        ob, oc = fix.take3(4, TT), fix.take3(4, TT)
        gt = fix.take3(6, TT)
        ml_at = fix.at
        mq, mk = fix.take3(4, TT)[0:64], fix.take3(4, TT)[0:64]
        mv, mo = fix.take3(4, TT), fix.take3(4, TT)
        ckv, kr, rot = fix.take(TT), fix.take(TT), fix.take(2 * TT)
        cq = fix.take3(2, TT)
        rows = fix.take3(10, TT)[0:4]
        R_G, R_B, R_EG, R_KD, R_BEG, R_W, R_M, R_INT, R_EMR, R_WK = range(10)
        mr = fix.take(TT)[0:4]
        g0 = fix.at

        ident = const[:, C_ID:C_ID + 128]
        ones = const[:, C_ONE:C_ONE + 128]
        inc_mask = const[:, C_INC:C_INC + 128]
        caus = const[:, C_CAUS:C_CAUS + 384]
        rope = const[:, C_ROPE:C_ROPE + TT]

        r = Region(arena, g0, ARENA)
        ci = r.take3(12, 24 + 3 + TT)
        qkv = r.take3(16, TT)
        z = r.take3(4, TT)
        a0 = r.at
        aq = r.take(2048).rearrange("p (i t l) -> p i t l", i=8, t=2)
        tm, tt, ym = r.take3(8, 128), r.take3(8, 128), r.take3(8, 128)
        s_at = r.at
        S = r.take3(NS, 128)
        scr = r.take(6 * TT)
        cvr = scr[:, 0:3 * TT].rearrange("p (k n) -> p k n", k=3)
        thr = scr[:, 3 * TT:].rearrange("p (k n) -> p k n", k=3)
        vd = scr[0:32, 0:1024].rearrange("p (i s n) -> p i s n", i=2, s=4)
        kvt = scr[0:32, 1024:1280]
        l2sq = arena[:, a0:a0 + 8 * TT].rearrange("p (k n) -> p k n", k=8)
        l2rt = arena[:, a0 + 8 * TT:a0 + 16 * TT].rearrange("p (k n) -> p k n", k=8)
        nsq, nrt = l2sq[:, 0:4, :], l2sq[:, 4:8, :]
        xsq, rms = l2sq, l2rt[:, 0, :]
        rt = arena[:, ml_at:ml_at + 8 * TT].rearrange("p (k n) -> p k n", k=8)[0:4]
        c = Region(arena, g0, g0 + 12 * 291)
        kdt, bv, vn, s1 = c.take3(8, 128), c.take3(8, 128), c.take3(4, 128), c.take3(4, 128)
        qe = r.take3(4, 128)
        cols = r.take(48)
        bes, egl = r.take3(4, 8), r.take3(4, 9)
        cvs, ths = r.take3(12, 8), r.take3(12, 8)
        sm = [r.take3(4, 8) for _ in range(8)]
        m0s, nml, ea = r.take(8)[0:4], r.take(2)[0:4], r.take(1)[0:4]
        co = r.take3(12, 27)
        o = Region(arena, ob_at, ob_at + 8 * TT)
        dec = o.take3(8, 128)
        am = o.take(1024).rearrange("p (c h l) -> p c h l", c=2, h=4)
        ends = [r.at]

        r = Region(arena, g0, s_at)
        emr = r.take3(4, TT)
        vt = r.take3(8, 129)
        kw = r.take3(8, 64)
        dm, pt = r.take3(8, 128), r.take3(8, 128)
        qs, c1 = r.take3(4, 128)[0:64], r.take3(4, 129)[0:64]
        den = r.take3(4, 128)
        ims, wks = r.take3(4, 9), r.take3(4, 8)
        mn = r.take(NS)[0:64]
        ms = [r.take3(4, 8) for _ in range(8)]
        csq, crt = r.take3(4, TT), r.take3(4, TT)
        mcols = cols
        ends.append(r.at)
        C = arena[0:64, s_at:s_at + NS * 128].rearrange("p (s n) -> p s n", s=NS)

        r = Region(arena, g0, ARENA)
        wuq = r.take(2048).rearrange("p (k h n) -> p k h n", k=2, h=8)
        wuk, wukt, wuv = r.take3(8, 64), r.take3(8, 128)[0:64], r.take(512)
        asq, art = r.take3(3, TT), r.take3(2, TT)
        cqn, ckn = r.take3(2, TT), r.take(TT)
        qf, kf = r.take3(8, TT), r.take3(8, TT)
        va = r.take3(2, 512)
        ql = r.take3(8, 8)
        qrb = r.take(256).rearrange("p (b r h) -> p b r h", b=8, r=4)
        pr1, pr2, snew = r.take3(8, 8), r.take3(8, 8), r.take3(8, 8)
        mx, nmx, smm = r.take3(2, 8), r.take3(2, 8), r.take3(2, 8)
        p_at = r.at
        ss, ptt = r.take3(8, 384), r.take3(24, 128)
        ends.append(r.at)
        r = Region(arena, p_at, ARENA)
        lat = r.take3(2, 2560)
        ltt = r.take3(16, 128)
        krt = r.take3(4, 128)
        ssb = r.take3(16, 8)
        pb = r.take(256).rearrange("p (i r h) -> p i r h", i=2, r=16)
        bm, bs = r.take3(2, 8), r.take3(2, 8)
        mxb, pn, rd = r.take3(2, 8), r.take3(2, 8), r.take3(2, 8)
        mx8 = r.take(1)[0:8]
        ctxs = r.take3(8, 8)
        ends.append(r.at)

        mg = arena[:, ml_at:ml_at + 8 * TT].rearrange("p (k n) -> p k n", k=8)
        r = Region(arena, g0, a0)
        hid = r.take3(FFC, TT)
        fc = r.take3(3, 258)
        r = Region(arena, a0 + 16 * TT, ARENA)
        fcv, fth = r.take3(3, 256), r.take3(3, 256)
        fs = r.take3(FFC, 24)
        us, fcs, fts = r.take3(FFC, 8), r.take3(FFC, 8), r.take3(FFC, 8)
        fo = r.take3(FFC, 18)
        mt = r.take3(2, TT)
        ends.append(r.at)
        assert max(ends) <= ARENA

        def sem(name):
            return ctx.enter_context(nc.semaphore(name))

        w_landed = [sem(f"w_landed{i}") for i in range(SLOTS)]
        w_started = sem("w_started")
        out_ready = sem("out_ready")
        read_by = {"A": sem("read_by_scalar"), "V": sem("read_by_vector")}
        own = {e: sem(f"own_{e}") for e in ("act", "dve", "pool")}
        const_in, x_in, idx_ready = sem("const_in"), sem("x_in"), sem("idx_ready")
        first_rows = sem("first_rows")
        layer_open = sem("layer_open")
        spare = {e: sem(f"spare_{e}") for e in ("pe", "pool")}
        last_squares, last_root, last_norm, y_out = sem("last_squares"), sem("last_root"), sem("last_norm"), sem("y_out")
        last_sum = sem("last_sum")
        signal = {n: sem(n) for n in SIGNALS}
        given = {n: 0 for n in SIGNALS}
        NOUT = len(SCHED)

        def at(l, name, k):
            return signal[name], l * SIGNALS[name] + k

        def up(name, n=1):
            given[name] += n
            return signal[name], n

        def out(l, name, i=0):
            return out_ready, l * NOUT + WHERE[name, i] + 1

        def evac(l, name, i=0):
            reader, k = RANK[name, i]
            return read_by[reader], l * len(READS[reader]) + k + 1

        reads = {"A": 0, "V": 0}

        def read(name, i=0):
            reader, k = RANK[name, i]
            assert reads[reader] == k, (name, i, READS[reader][reads[reader]])
            reads[reader] += 1
            return read_by[reader], 1

        def bank(name, i=0):
            return banks[:, WHERE[name, i] % 8, :]

        def heads(ap, n):
            return ap.rearrange("p (h n) -> p h n", n=n)

        OWN = dict(act=400, dve=500, pool=120)

        def stepper(eng, which, l):
            count = [0]

            def link(ins):
                count[0] += 1
                ins.then_inc(own[which], 1)
                eng.wait_ge(own[which], l * OWN[which] + count[0])

            def close():
                assert count[0] < OWN[which]
                eng.sem_inc(own[which], OWN[which] - count[0])

            return link, close

        block = ctx.enter_context(nc.Block())

        @block.sync
        def _(sp):
            units = a["weights"]
            for s in range(SLOTS):
                sp.dma_start(ring[:, s * 1024:(s + 1) * 1024], units[s]).then_inc(w_landed[s], 16)
            with sp.Fori(1, L * UNITS // SLOTS) as g:
                for s in range(SLOTS):
                    sp.wait_ge(w_started, g * SLOTS + (s - SLOTS + 2))
                    sp.dma_start(ring[:, s * 1024:(s + 1) * 1024],
                                 units[bass.ds(g * SLOTS + s, 1)].rearrange("a p n -> p (a n)")).then_inc(w_landed[s], 16)

        @block.tensor
        def _(pe):
            with pe.Fori(0, L) as l:
                order, tile = [0], [0]

                def claim(name, i=0, *operands):
                    assert SCHED[order[0]][:2] == (name, i), (SCHED[order[0]], name, i)
                    before = (SCHED[order[0] - 8][:2],) if order[0] >= 8 else ()
                    last = {}
                    for group in before + operands:
                        reader, k = RANK[group]
                        last[reader] = max(last.get(reader, 0), k + 1)
                    if "A" in last:
                        pe.wait_ge(read_by["A"], l * len(READS["A"]) + last["A"])
                    if "V" in last:
                        pe.wait_ge(read_by["V"], l * len(READS["V"]) + last["V"])
                    order[0] += 1
                    return bank(name, i)

                def weights(dst, rhs, k):
                    for j in range(k):
                        unit, part = divmod(tile[0], 8)
                        slot = unit % SLOTS
                        if part == 0:
                            pe.wait_ge(w_landed[slot], l * (16 * UNITS // SLOTS) + 16 * (unit // SLOTS + 1))
                        at_ = slot * 1024 + part * 128
                        mm = nc.tensor.matmul(dst, ring[:, at_:at_ + 128], rhs[:, j, :], start=(j == 0), stop=(j == k - 1))
                        if part == 0:
                            assert j < k - 1
                            mm.then_inc(w_started, 1)
                        tile[0] += 1
                    return mm

                def project(name, i, rhs, k=KT, *operands):
                    weights(claim(name, i, *operands)[:, 0:TT], rhs, k).then_inc(out_ready, 1)

                def plain():
                    pe.sem_inc(spare["pe"], 1)

                fills = [("pm", i) for i in range(12)] + [("pa", i) for i in range(4)]

                def fill(n):
                    for _ in range(n):
                        project(*fills.pop(0), hn)

                def sums(name, i, parts):
                    b = claim(name, i)
                    for j, s in enumerate(parts):
                        mm = nc.tensor.matmul(b[:, 0:TT], ones, s, start=(j == 0), stop=(j == len(parts) - 1))
                    mm.then_inc(out_ready, 1)

                pe.wait_ge(const_in, 16)
                pe.wait_ge(*at(l, "squares", 1))
                sums("n1", 0, [xsq[:, k, :] for k in range(KT)])
                pe.wait_ge(*at(l, "hidden_norm", 1))
                project("pS", 0, hn)
                for j in range(12):
                    project("pq", j, hn)
                for j in range(4):
                    project("pz", j, hn)
                pe.wait_ge(*at(l, "qk_squares", 1))
                for i in range(8):
                    sums("l2", i, [l2sq[:, i, :]])
                pe.wait_ge(*at(l, "rows_act", 1))
                pe.wait_ge(*at(l, "rows_dve", 1))
                b = claim("rowT")
                plain()
                for c_ in range(NCH):
                    for q, row in enumerate((R_G, R_B, R_KD, R_BEG, R_W, R_WK)):
                        mm = nc.tensor.transpose(b[:, (c_ * 6 + q) * 4:(c_ * 6 + q) * 4 + 4],
                                                 rows[:, row, c_ * P:(c_ + 1) * P], ident[0:4, 0:4])
                mm.then_inc(out_ready, 1)

                def spread(name, h, row):
                    b = claim(name, h)
                    nc.tensor.matmul(b[:, 0:TT], ident[0:4, h:h + 1].to_broadcast((4, P)), rows[:, row, :],
                                     start=True, stop=True).then_inc(out_ready, 1)

                for h in range(NH):
                    spread("bcB", h, R_B)
                    spread("bcG", h, R_G)
                    spread("bcE", h, R_EG)
                fill(2)
                pe.wait_ge(*at(l, "qk_unit", 1))
                for c_ in range(NCH):
                    b = claim("kT", c_)
                    for h in range(NH):
                        mm = nc.tensor.transpose(b[:, h * P:(h + 1) * P], qkv[:, 4 + h, c_ * P:(c_ + 1) * P], ident)
                    mm.then_inc(out_ready, 1)
                for c_ in range(NCH):
                    b = claim("vT", c_)
                    for h in range(NH):
                        mm = nc.tensor.transpose(b[:, h * P:(h + 1) * P], qkv[:, 8 + h, c_ * P:(c_ + 1) * P], ident)
                    mm.then_inc(out_ready, 1)
                for i in range(8):
                    c_, h = divmod(i, NH)
                    b = claim("aq", i, ("bcB", h), ("bcE", h))
                    nc.tensor.matmul(heads(b[:, 0:256], P), qkv[:, 4 + h, c_ * P:(c_ + 1) * P],
                                     qkv[:, h:h + 13:12, c_ * P:(c_ + 1) * P], start=True, stop=True).then_inc(out_ready, 1)
                for j in range(LEVELS):
                    for c_ in range(NCH):
                        i = 2 * j + c_
                        pe.wait_ge(*at(l, "level_a", i + 1))
                        b = claim("Y", i, ("T", i - 2)) if j else claim("Y", i)
                        for h in range(NH):
                            mm = nc.tensor.matmul(b[:, h * P:(h + 1) * P], am[:, c_, h, :],
                                                  ident if j == 0 else tm[:, 4 * c_ + h, :], start=True, stop=True)
                        mm.then_inc(out_ready, 1)
                    if j < LEVELS - 1:
                        for c_ in range(NCH):
                            i = 2 * j + c_
                            b = claim("T", i, ("Y", i), ("TT", i - 2)) if j else claim("T", i, ("Y", i))
                            for h in range(NH):
                                mm = nc.tensor.matmul(b[:, h * P:(h + 1) * P], ident if j == 0 else tt[:, 4 * c_ + h, :],
                                                      ym[:, 4 * c_ + h, :], start=True, stop=True)
                            mm.then_inc(out_ready, 1)
                    for c_ in range(NCH):
                        i = 2 * j + c_
                        b = claim("TT", i, ("Y", i), ("TT", i - 2)) if j else claim("TT", i, ("Y", i))
                        for h in range(NH):
                            mm = nc.tensor.matmul(b[:, h * P:(h + 1) * P], ym[:, 4 * c_ + h, :],
                                                  ident if j == 0 else tt[:, 4 * c_ + h, :], start=True, stop=True)
                        mm.then_inc(out_ready, 1)
                    fill(1)
                b = claim("vn0", 0, ("TT", 2 * LEVELS - 1), ("vT", 1))
                for h in range(NH):
                    mm = nc.tensor.matmul(b[:, h * P:(h + 1) * P], tt[:, h, :], bv[:, h, :], start=True, stop=True)
                mm.then_inc(out_ready, 1)
                b = claim("o0", 0, ("vn0", 0))
                for h in range(NH):
                    mm = nc.tensor.matmul(b[:, h * P:(h + 1) * P], vn[:, h, :], aq[:, h, 0, :], start=True, stop=True)
                mm.then_inc(out_ready, 1)
                b = claim("s1")
                for h in range(NH):
                    mm = nc.tensor.matmul(b[:, h * P:(h + 1) * P], kdt[:, h, :], vn[:, h, :], start=True, stop=True)
                mm.then_inc(out_ready, 1)
                fill(1)
                b = claim("ks", 0, ("s1", 0))
                for h in range(NH):
                    mm = nc.tensor.matmul(b[:, h * P:(h + 1) * P], qkv[:, 4 + h, P:TP], s1[:, h, :], start=True, stop=True)
                mm.then_inc(out_ready, 1)
                fill(1)
                b = claim("vn1", 0, ("ks", 0))
                for h in range(NH):
                    mm = nc.tensor.matmul(b[:, h * P:(h + 1) * P], tt[:, 4 + h, :], bv[:, h, :], start=True, stop=True)
                mm.then_inc(out_ready, 1)
                b = claim("o1", 0, ("vn1", 0))
                for h in range(NH):
                    nc.tensor.matmul(b[:, h * P:(h + 1) * P], s1[:, h, :], qe[:, h, :], start=True, stop=False)
                    mm = nc.tensor.matmul(b[:, h * P:(h + 1) * P], vn[:, h, :], aq[:, 4 + h, 0, :], start=False, stop=True)
                mm.then_inc(out_ready, 1)
                b = claim("s2")
                for h in range(NH):
                    mm = nc.tensor.matmul(b[:, h * P:(h + 1) * P], kdt[:, 4 + h, :], vn[:, h, :], start=True, stop=True)
                mm.then_inc(out_ready, 1)
                pe.wait_ge(*at(l, "s_loaded", 16))
                b = claim("sk")
                for h in range(NH):
                    for n in range(NB):
                        mm = nc.tensor.matmul(b[:, 2 * (h * NB + n):2 * (h * NB + n) + 2], S[:, h * NB + n, :],
                                              qkv[:, h:h + 5:4, TP + n], start=True, stop=True)
                mm.then_inc(out_ready, 1)
                pe.wait_ge(*at(l, "sample_prods", 1))
                b = claim("qk")
                nc.tensor.matmul(heads(b[:, 0:NS], NB), ones, sm[0], start=True, stop=True).then_inc(out_ready, 1)
                fill(2)

                def rows_of(name, k_, v_, ready, dk):
                    pe.wait_ge(*at(l, ready, 1))
                    b = claim(name)
                    plain()
                    nc.tensor.transpose(b[0:NS, 0:dk], k_, ident[0:dk, 0:dk])
                    nc.tensor.transpose(b[0:NS, P:2 * P], v_, ident).then_inc(out_ready, 1)

                def outer(name, ready, dk, rows_group):
                    for j in range(8):
                        pe.wait_ge(*at(l, ready, j + 1))
                        b = claim(name, j, rows_group)
                        nc.tensor.matmul(b[0:dk, :], kvt[:, 0:dk], vd[:, j % 2].rearrange("p s n -> p (s n)"),
                                         start=True, stop=True).then_inc(out_ready, 1)

                rows_of("kvT", sm[1].rearrange("p h n -> p (h n)"), sm[2].rearrange("p h n -> p (h n)"), "sample_vnew", P)
                outer("out", "v_diag", P, ("kvT", 0))
                pe.wait_ge(*at(l, "oa_squares", 1))
                for i in range(4):
                    sums("na", i, [nsq[:, i, :]])
                fill(3)

                for h in range(NH):
                    spread("bcM", h, R_M)
                    spread("bcI", h, R_INT)
                    spread("bcR", h, R_EMR)
                b = claim("bcW")
                for h in range(NH):
                    mm = nc.tensor.matmul(b[:, h * NB:(h + 1) * NB], ident[0:4, h:h + 1].to_broadcast((4, P)),
                                          rows[:, R_WK, TP:TT], start=True, stop=True)
                mm.then_inc(out_ready, 1)
                for c_ in range(NCH):
                    b = claim("mkT", c_, ("pm", 3))
                    plain()
                    for h in range(NH):
                        mm = nc.tensor.transpose(b[:, h * 64:(h + 1) * 64], mk[:, h, c_ * P:(c_ + 1) * P], ident[0:64, 0:64])
                    mm.then_inc(out_ready, 1)
                for c_ in range(NCH):
                    b = claim("mvT", c_, ("pm", 7))
                    for h in range(NH):
                        mm = nc.tensor.transpose(b[:, h * P:(h + 1) * P], mv[:, h, c_ * P:(c_ + 1) * P], ident)
                    mm.then_inc(out_ready, 1)
                for c_ in range(NCH):
                    b = claim("mqk", c_)
                    for h in range(NH):
                        mm = nc.tensor.matmul(b[:, h * P:(h + 1) * P], mk[:, h, c_ * P:(c_ + 1) * P],
                                              mq[:, h, c_ * P:(c_ + 1) * P], start=True, stop=True)
                    mm.then_inc(out_ready, 1)
                b = claim("md0", 0, ("mqk", 0))
                nc.tensor.matmul(b, ones, pt[:, 0:4, :], start=True, stop=True).then_inc(out_ready, 1)
                pe.wait_ge(*at(l, "ones_column", 1))
                b = claim("mn0", 0, ("mvT", 1))
                for h in range(NH):
                    mm = nc.tensor.matmul(b[:, h * P:(h + 1) * P], vt[:, h, 0:P], pt[:, h, :], start=True, stop=True)
                mm.then_inc(out_ready, 1)
                for i in range(2):
                    b = claim("mc1", i)
                    for j in range(2):
                        h = 2 * i + j
                        mm = nc.tensor.matmul(b[0:64, j * 129:(j + 1) * 129], kw[:, h, :], vt[:, h, :], start=True, stop=True)
                    mm.then_inc(out_ready, 1)
                b = claim("md1", 0, ("mqk", 1), ("mc1", 1))
                for h in range(NH):
                    nc.tensor.matmul(b[:, h * P:(h + 1) * P], c1[:, h, P:P + 1].to_broadcast((64, P)), qs[:, h, :],
                                     start=True, stop=False)
                    mm = nc.tensor.matmul(b[:, h * P:(h + 1) * P], ones, pt[:, 4 + h, :], start=False, stop=True)
                mm.then_inc(out_ready, 1)
                b = claim("mn1")
                for h in range(NH):
                    nc.tensor.matmul(b[:, h * P:(h + 1) * P], c1[:, h, 0:P], qs[:, h, :], start=True, stop=False)
                    mm = nc.tensor.matmul(b[:, h * P:(h + 1) * P], vt[:, 4 + h, 0:P], pt[:, 4 + h, :], start=False, stop=True)
                mm.then_inc(out_ready, 1)
                for i in range(2):
                    b = claim("mc2", i)
                    for j in range(2):
                        h = 2 * i + j
                        mm = nc.tensor.matmul(b[0:64, j * 129:(j + 1) * 129], kw[:, 4 + h, :], vt[:, 4 + h, :], start=True, stop=True)
                    mm.then_inc(out_ready, 1)
                pe.wait_ge(*at(l, "c_loaded", 16))
                b = claim("mq")
                for h in range(NH):
                    for n in range(NB):
                        mm = nc.tensor.matmul(b[:, h * NB + n:h * NB + n + 1], C[:, h * NB + n, :],
                                              mq[:, h, TP + n:TP + n + 1], start=True, stop=True)
                mm.then_inc(out_ready, 1)
                pe.wait_ge(*at(l, "msample_prods", 1))
                b = claim("mqn")
                nc.tensor.matmul(heads(b[:, 0:NS], NB), ones[0:64, :], ms[0][0:64], start=True, stop=True)
                nc.tensor.matmul(heads(b[:, NS:2 * NS], NB), ones[0:64, :], ms[1][0:64], start=True, stop=True).then_inc(out_ready, 1)
                rows_of("mkvT", ms[2][0:64].rearrange("p h n -> p (h n)"), ms[3].rearrange("p h n -> p (h n)"), "msample_kv", 64)
                outer("mout", "mv_diag", 64, ("mkvT", 0))
                pe.wait_ge(*at(l, "oc_squares", 1))
                for i in range(4):
                    sums("nc", i, [csq[:, i, :]])

                pe.wait_ge(*at(l, "mla_loaded", 16))
                pe.wait_ge(*at(l, "latent_squares", 1))
                sums("nk", 0, [asq[:, 0, :]])
                sums("nq", 0, [asq[:, 1, :], asq[:, 2, :]])
                pe.wait_ge(*at(l, "latent_norm", 1))
                for h in range(MH):
                    b = claim("uq", h)
                    for k in range(2):
                        mm = nc.tensor.matmul(b[:, 0:TT], wuq[:, k, h, :], cqn[:, k, :], start=(k == 0), stop=(k == 1))
                    mm.then_inc(out_ready, 1)
                for i in range(4):
                    b = claim("uk", i)
                    for j in range(2):
                        mm = nc.tensor.matmul(b[0:64, j * TP:(j + 1) * TP], wuk[:, 2 * i + j, :], ckn[:, 0:TP], start=True, stop=True)
                    mm.then_inc(out_ready, 1)
                for c_ in range(NCH):
                    b = claim("uv", c_)
                    nc.tensor.matmul(b, ckn[:, c_ * P:(c_ + 1) * P], wuv, start=True, stop=True).then_inc(out_ready, 1)
                b = claim("ql", 0, ("uq", 7))
                for h in range(MH):
                    mm = nc.tensor.matmul(b[:, h * NB:(h + 1) * NB], wukt[:, h, :], qf[0:64, h, TP:TT], start=True, stop=True)
                mm.then_inc(out_ready, 1)
                pe.wait_ge(*at(l, "key_copied", 1))
                for h in range(MH):
                    b = claim("sc", h, ("uk", 3), ("uq", h))
                    nc.tensor.matmul(b[:, 0:P], qf[0:96, h, 0:P], kf[0:96, h, 0:P], start=True, stop=True)
                    nc.tensor.matmul(b[:, P:3 * P], qf[0:96, h, P:TP], kf[0:96, h, 0:TP], start=True, stop=True).then_inc(out_ready, 1)
                pe.wait_ge(*at(l, "probs", 1))
                for g in range(6):
                    b = claim("ptT", g)
                    for i in range(4 * g, 4 * g + 4):
                        h, t = divmod(i, 3)
                        mm = nc.tensor.transpose(b[:, (i % 4) * P:(i % 4 + 1) * P], ss[:, h, t * P:(t + 1) * P], ident)
                    mm.then_inc(out_ready, 1)
                for i in range(4):
                    b = claim("pv", i, ("ptT", 5), ("uv", 1))
                    for j in range(2):
                        h = 2 * i + j
                        v0, v1 = (va[:, c_, h * 64:(h + 1) * 64] for c_ in range(NCH))
                        nc.tensor.matmul(b[0:64, j * TP:j * TP + P], v0, ptt[:, 3 * h, :], start=True, stop=True)
                        nc.tensor.matmul(b[0:64, j * TP + P:(j + 1) * TP], v0, ptt[:, 3 * h + 1, :], start=True, stop=False)
                        mm = nc.tensor.matmul(b[0:64, j * TP + P:(j + 1) * TP], v1, ptt[:, 3 * h + 2, :], start=False, stop=True)
                    mm.then_inc(out_ready, 1)
                pe.wait_ge(*at(l, "new_prods", 1))
                b = claim("sn")
                nc.tensor.matmul(heads(b[:, 0:64], 8), ones, pr1, start=True, stop=False)
                nc.tensor.matmul(heads(b[:, 0:64], 8), ones[64:96, :], pr2[64:96], start=False, stop=True).then_inc(out_ready, 1)
                pe.wait_ge(*at(l, "query_blocks", 1))
                for n in range(NB + 1):
                    if n < NB:
                        la = lat[:, n % 2, :]
                        pe.wait_ge(*at(l, f"lat_in{n % 2}", 32 * (n // 2 + 1)))
                        b = claim("krT", n)
                        for q in range(4):
                            mm = nc.tensor.transpose(b[:, q * P:(q + 1) * P], la[:, 2048 + q * P:2048 + (q + 1) * P], ident)
                        mm.then_inc(out_ready, 1)
                        for q in range(4):
                            b = claim("ltr", 4 * n + q)
                            for k in range(4):
                                rr = 4 * q + k
                                mm = nc.tensor.transpose(b[:, k * P:(k + 1) * P], la[:, rr * P:(rr + 1) * P], ident)
                            mm.then_inc(out_ready, 1)
                        b = claim("ss", n, ("krT", n), ("ltr", 4 * n + 2), ("ltr", 4 * n + 3))
                        for q in range(4):
                            nc.tensor.matmul(b[:, q * 32:(q + 1) * 32], krt[:, q, :], qrb[:, n].rearrange("p r h -> p (r h)"),
                                             start=True, stop=True, skip_group_check=True)
                            for k in range(4):
                                rr = 4 * q + k
                                mm = nc.tensor.matmul(b[:, rr * 8:(rr + 1) * 8], ltt[:, rr, :], ql[:, :, n],
                                                      start=False, stop=True, skip_group_check=True)
                        mm.then_inc(out_ready, 1)
                    if n > 0:
                        m, la = n - 1, lat[:, (n - 1) % 2, :]
                        pe.wait_ge(*at(l, "page_sums", n))
                        b = claim("cs", m)
                        for rr in range(NR):
                            nc.tensor.matmul(b[:, 0:8], la[:, rr * P:(rr + 1) * P], pb[:, m % 2, rr, :], start=(rr == 0), stop=(rr == NR - 1))
                        nc.tensor.matmul(b[:, 8:16], ones, bs[:, m % 2, :], start=True, stop=True).then_inc(out_ready, 1)
                    if n < NB:
                        pe.wait_ge(*at(l, "page_max", n + 1))
                        b = claim("mxT", n)
                        plain()
                        nc.tensor.transpose(b[0:8, 0:P], bm[:, n % 2, :], ident).then_inc(out_ready, 1)
                        b = claim("mxB", n, ("mxT", n))
                        nc.tensor.matmul(b[:, 0:8], mx8.to_broadcast((8, P)), ident[0:8, 0:8], start=True, stop=True).then_inc(out_ready, 1)
                b = claim("ov", 0, ("cs", NB - 1))
                for h in range(MH):
                    mm = nc.tensor.matmul(b[0:64, h * NB:(h + 1) * NB], wuv[:, h * 64:(h + 1) * 64], ctxs[:, h, :], start=True, stop=True)
                mm.then_inc(out_ready, 1)

                pe.wait_ge(*at(l, "oa_done", 1))
                pe.wait_ge(*at(l, "oc_done", 1))
                for n in range(8):
                    for i in range(3):
                        project("pg", 3 * n + i, hn)
                    for i, br in enumerate((oa, ob, oc)):
                        project("pb", 3 * n + i, br, 4, ("ov", 0))
                pe.wait_ge(*at(l, "merged", 8))
                for n in range(8):
                    project("pw", n, mg)
                pe.wait_ge(*at(l, "squares", 2))
                sums("n2", 0, [xsq[:, k, :] for k in range(KT)])
                pe.wait_ge(*at(l, "hidden_norm", 2))
                for j in range(FFC):
                    project("fg", j, hn)
                    project("fu", j, hn)
                pe.wait_ge(*at(l, "hidden", 1))
                for n in range(8):
                    project("fd", n, hid, FFC)
                assert order[0] == NOUT and tile[0] == UNITS * 8 and not fills
            pe.wait_ge(last_squares, 1)
            for k in range(KT):
                mm = nc.tensor.matmul(banks[:, 0, 0:TT], ones, xsq[:, k, :], start=(k == 0), stop=(k == KT - 1))
            mm.then_inc(last_sum, 1)

        @block.scalar
        def _(act):
            reads["A"] = 0
            A = nc.scalar.activation
            act.wait_ge(const_in, 16)
            act.wait_ge(x_in, 16)
            with act.Fori(0, L) as l:
                link, close = stepper(act, "act", l)

                def copy(dst, src, scale=1.0):
                    return A(dst, src, ACT.Copy, scale=scale)

                def fill(name, i):
                    b = bank(name, i)
                    act.wait_ge(*out(l, name, i))
                    if name == "pm" and i < 4:
                        dst, scale = (mq, 1.0) if i < 2 else (mk, 0.125)
                        copy(dst[:, 2 * (i % 2), :], b[0:64, 0:TT], scale)
                        last = copy(dst[:, 2 * (i % 2) + 1, :], b[64:128, 0:TT], scale)
                    elif name == "pm" and i < 8:
                        last = copy(mv[:, i - 4, :], b[:, 0:TT])
                    elif name == "pm":
                        last = A(mo[:, i - 8, :], b[:, 0:TT], ACT.Tanh, scale=0.5)
                    elif i == 0:
                        last = copy(ckv, b[:, 0:TT])
                    else:
                        last = copy(cq[:, i - 2, :], b[:, 0:TT])
                    last.then_inc(*read(name, i))

                act.wait_ge(layer_open, l + 1)
                A(xsq, x, ACT.Square).then_inc(*up("squares"))
                act.wait_ge(*out(l, "n1"))
                A(rms, bank("n1")[:, 0:TT], ACT.Sqrt, scale=1.0 / D, bias=EPS).then_inc(*read("n1"))
                act.wait_ge(*out(l, "pS"))
                A(rows[:, R_B, :], bank("pS")[32:36, 0:TT], ACT.Tanh, scale=0.5).then_inc(*up("beta_tanh"))
                act.wait_ge(*at(l, "par_loaded", 16))
                for j in range(14):
                    if j < 12:
                        act.wait_ge(*out(l, "pq", j))
                        copy(ci[:, j, 27:27 + TT], bank("pq", j)[:, 0:TT]).then_inc(*read("pq", j))
                    if j >= 2:
                        act.wait_ge(*at(l, "conv", j - 1))
                        if j >= 5:
                            act.wait_ge(*at(l, "silu", j - 4))
                        A(thr[:, (j - 2) % 3, 0:TP], cvr[:, (j - 2) % 3, 0:TP], ACT.Tanh, scale=0.5).then_inc(*up("conv_tanh"))
                    if j == 3:
                        act.wait_ge(*at(l, "row_x", 1))
                        link(A(rt[:, 2:4, :], rt[:, 0:2, :], ACT.Abs))
                        A(rt[:, 2:4, :], rt[:, 2:4, :], ACT.Exp, scale=-1.0).then_inc(*up("row_e"))
                        A(ea, par[0:4, Q_ROW:Q_ROW + 1], ACT.Exp).then_inc(*up("row_ea"))
                    if j == 5:
                        act.wait_ge(*at(l, "row_u", 1))
                        A(rows[:, R_M:R_M + 2, :], rt[:, 4:6, :], ACT.Ln).then_inc(*up("row_ln"))
                    if j == 10:
                        act.wait_ge(*at(l, "row_m", 1))
                        link(A(rows[:, R_EG, :], rows[:, R_G, :], ACT.Exp))
                        act.wait_ge(*at(l, "row_m0", 1))
                        for c_ in range(NCH):
                            s = slice(c_ * P, (c_ + 1) * P)
                            e = c_ * P + P - 1
                            A(rows[:, R_KD, s], rows[:, R_G, s], ACT.Exp, scale=-1.0, bias=rows[:, R_G, e:e + 1])
                            A(rows[:, R_WK, s], rows[:, R_W, s], ACT.Exp, bias=nml[:, c_:c_ + 1])
                        A(rows[:, R_INT, 0:P], rows[:, R_M, 0:P], ACT.Exp, scale=-1.0)
                        A(rows[:, R_INT, P:TP], rows[:, R_M, P:TP], ACT.Exp, scale=-1.0, bias=mr[:, P - 1:P])
                        A(rows[:, R_INT, TP:TT], rt[:, 3, 0:NB], ACT.Exp)
                        A(rows[:, R_WK, TP:TT], rt[:, 3, NB:2 * NB], ACT.Exp)
                        A(rows[:, R_EMR, :], mr, ACT.Exp, scale=-1.0).then_inc(*up("rows_act"))
                act.wait_ge(*at(l, "sconv", 1))
                A(ths, cvs, ACT.Tanh, scale=0.5).then_inc(*up("sconv_tanh"))
                for j in range(4):
                    act.wait_ge(*out(l, "pz", j))
                    A(z[:, j, :], bank("pz", j)[:, 0:TT], ACT.Tanh, scale=0.5).then_inc(*up("z_tanh"))
                act.wait_ge(*at(l, "silu", 13))
                A(l2sq, qkv[:, 0:8, :], ACT.Square).then_inc(*up("qk_squares"))
                for i in range(8):
                    sc = float(P) if i < 4 else 1.0
                    act.wait_ge(*out(l, "l2", i))
                    A(l2rt[:, i, :], bank("l2", i)[:, 0:TT], ACT.Sqrt, scale=sc, bias=4 * EPS * sc).then_inc(*read("l2", i))
                act.wait_ge(*at(l, "rows_dve", 1))
                fill("pm", 0)
                fill("pm", 1)
                act.wait_ge(*at(l, "decay_in", 4))
                A(dec, dec, ACT.Exp).then_inc(*up("decay_exp"))
                act.wait_ge(*at(l, "conv_state", 1))
                act.wait_ge(*evac(l, "rowT"))
                for c_ in range(NCH):
                    act.wait_ge(*out(l, "kT", c_))
                    for h in range(NH):
                        k = (c_ * 6 + 2) * 4 + h
                        last = copy(kdt[:, 4 * c_ + h, :], bank("kT", c_)[:, h * P:(h + 1) * P], cols[:, k:k + 1])
                    last.then_inc(*read("kT", c_))
                n = 2
                for j in range(LEVELS):
                    for c_ in range(NCH):
                        i = 2 * j + c_
                        act.wait_ge(*out(l, "Y", i))
                        copy(ym[:, 4 * c_:4 * c_ + 4, :], heads(bank("Y", i), P)).then_inc(*read("Y", i))
                    fill("pm", n)
                    n += 1
                act.wait_ge(*out(l, "vn0"))
                copy(vn, heads(bank("vn0"), P)).then_inc(*read("vn0"))
                act.wait_ge(*out(l, "o0"))
                copy(oa[:, :, 0:P], heads(bank("o0"), P)).then_inc(*read("o0"))
                act.wait_ge(*out(l, "s1"))
                copy(s1, heads(bank("s1"), P)).then_inc(*read("s1"))
                fill("pm", 9)
                fill("pm", 10)
                act.wait_ge(*out(l, "vn1"))
                copy(vn, heads(bank("vn1"), P), -1.0).then_inc(*read("vn1"))
                act.wait_ge(*out(l, "o1"))
                copy(oa[:, :, P:TP], heads(bank("o1"), P)).then_inc(*read("o1"))
                fill("pm", 11)
                fill("pa", 0)
                act.wait_ge(*out(l, "kvT"))
                copy(kvt, bank("kvT")[0:NS, 0:2 * P]).then_inc(*read("kvT"))
                act.wait_ge(*evac(l, "qk"))
                act.wait_ge(*evac(l, "o1"))
                A(nsq, oa, ACT.Square).then_inc(*up("oa_squares"))
                for i in range(4):
                    act.wait_ge(*out(l, "na", i))
                    A(nrt[:, i, :], bank("na", i)[:, 0:TT], ACT.Sqrt, scale=4.0 / P, bias=4 * EPS).then_inc(*read("na", i))
                fill("pa", 2)
                fill("pa", 3)

                act.wait_ge(*at(l, "oa_done", 1))
                act.wait_ge(*at(l, "st_ps", 16))
                for h in range(NH):
                    act.wait_ge(*out(l, "bcR", h))
                    copy(emr[:, h, :], bank("bcR", h)[:, 0:TT]).then_inc(*read("bcR", h))
                act.wait_ge(*at(l, "mdecay_in", 4))
                A(dm, dm, ACT.Exp, scale=-1.0).then_inc(*up("mdecay_exp"))
                for c_ in range(NCH):
                    act.wait_ge(*out(l, "mkT", c_))
                    for h in range(NH):
                        k = (c_ * 6 + 5) * 4 + h
                        last = copy(kw[:, 4 * c_ + h, :], bank("mkT", c_)[:, h * 64:(h + 1) * 64], cols[:, k:k + 1])
                    last.then_inc(*read("mkT", c_))
                for c_ in range(NCH):
                    act.wait_ge(*out(l, "mvT", c_))
                    copy(vt[:, 4 * c_:4 * c_ + 4, 0:P], heads(bank("mvT", c_), P)).then_inc(*read("mvT", c_))
                act.wait_ge(*out(l, "md0"))
                A(den, heads(bank("md0"), P), ACT.Abs).then_inc(*read("md0"))
                for i in range(2):
                    act.wait_ge(*out(l, "mc1", i))
                    copy(c1[:, 2 * i:2 * i + 2, :], bank("mc1", i)[0:64, 0:258].rearrange("p (h n) -> p h n", h=2)).then_inc(*read("mc1", i))
                act.wait_ge(*out(l, "md1"))
                act.wait_ge(*evac(l, "mn0"))
                A(den, heads(bank("md1"), P), ACT.Abs).then_inc(*read("md1"))
                act.wait_ge(*out(l, "mkvT"))
                copy(kvt[:, 0:64], bank("mkvT")[0:NS, 0:64])
                copy(kvt[:, P:2 * P], bank("mkvT")[0:NS, P:2 * P]).then_inc(*read("mkvT"))
                act.wait_ge(*at(l, "oc_raw", 1))
                A(csq, oc, ACT.Square).then_inc(*up("oc_squares"))
                for i in range(4):
                    act.wait_ge(*out(l, "nc", i))
                    A(crt[:, i, :], bank("nc", i)[:, 0:TT], ACT.Sqrt, scale=1.0 / P, bias=4 * EPS).then_inc(*read("nc", i))

                act.wait_ge(*at(l, "oc_done", 1))
                act.wait_ge(*at(l, "st_pc", 16))
                act.wait_ge(*at(l, "st_sn", 16))
                act.wait_ge(*at(l, "st_sc", 128))
                act.wait_ge(*at(l, "st_conv", 16))
                A(asq[:, 0, :], ckv, ACT.Square)
                act.wait_ge(*evac(l, "pa", 3))
                A(asq[:, 1:3, :], cq, ACT.Square).then_inc(*up("latent_squares"))
                act.wait_ge(*out(l, "nk"))
                A(art[:, 0, :], bank("nk")[:, 0:TT], ACT.Sqrt, scale=1.0 / P, bias=EPS).then_inc(*read("nk"))
                act.wait_ge(*out(l, "nq"))
                A(art[:, 1, :], bank("nq")[:, 0:TT], ACT.Sqrt, scale=1.0 / 256, bias=EPS).then_inc(*read("nq"))
                for i in range(4):
                    act.wait_ge(*out(l, "uk", i))
                    copy(kf[0:64, 2 * i:2 * i + 2, 0:TP], heads(bank("uk", i)[0:64], TP)).then_inc(*read("uk", i))
                for c_ in range(NCH):
                    act.wait_ge(*out(l, "uv", c_))
                    copy(va[:, c_, :], bank("uv", c_)).then_inc(*read("uv", c_))
                act.wait_ge(*out(l, "ql"))
                copy(ql, heads(bank("ql")[:, 0:64], 8)).then_inc(*read("ql"))
                act.wait_ge(*at(l, "neg_max", 1))
                for h in range(MH):
                    for t, s in enumerate((slice(0, P), slice(P, 3 * P))):
                        last = A(ss[:, h, s], ss[:, h, s], ACT.Exp, scale=SCALE, bias=nmx[:, t, h:h + 1], accum_out=smm[:, t, h:h + 1])
                last.then_inc(*up("probs_raw"))
                for g in range(6):
                    act.wait_ge(*out(l, "ptT", g))
                    copy(ptt[:, 4 * g:4 * g + 4, :], heads(bank("ptT", g), P)).then_inc(*read("ptT", g))
                for i in range(4):
                    act.wait_ge(*out(l, "pv", i))
                    copy(ob[0:64, i, 0:TP], bank("pv", i)[0:64, 0:TP])
                    copy(ob[64:128, i, 0:TP], bank("pv", i)[0:64, TP:2 * TP]).then_inc(*read("pv", i))
                for n in range(NB + 1):
                    if n < NB:
                        if n > 0:
                            act.wait_ge(*out(l, "ss", n - 1))
                        act.wait_ge(*out(l, "krT", n))
                        copy(krt, heads(bank("krT", n), P)).then_inc(*read("krT", n))
                        for q in (0, 2):
                            act.wait_ge(*out(l, "ltr", 4 * n + q))
                            copy(ltt[:, 4 * q:4 * q + 4, :], heads(bank("ltr", 4 * n + q), P)).then_inc(*read("ltr", 4 * n + q))
                    if n > 0:
                        act.wait_ge(*at(l, "page_sub", n))
                        A(pb[:, (n - 1) % 2], pb[:, (n - 1) % 2], ACT.Exp, scale=SCALE)
                        A(pn[:, (n - 1) % 2, :], pn[:, (n - 1) % 2, :], ACT.Exp, scale=SCALE).then_inc(*up("page_exp"))
                act.wait_ge(*out(l, "ov"))
                v = heads(bank("ov")[0:64, 0:64], 8)
                copy(ob[0:64, :, TP:TT], v[:, 0::2, :])
                copy(ob[64:128, :, TP:TT], v[:, 1::2, :]).then_inc(*read("ov"))

                for n in range(8):
                    for i in range(3):
                        k = 3 * n + i
                        act.wait_ge(*out(l, "pg", k))
                        if k >= 6:
                            act.wait_ge(*evac(l, "pb", k - 6))
                        A(gt[:, k % 6, :], bank("pg", k)[:, 0:TT], ACT.Tanh, scale=0.5).then_inc(*read("pg", k))
                act.wait_ge(*evac(l, "pw", 7))
                A(xsq, x, ACT.Square).then_inc(*up("squares"))
                act.wait_ge(*out(l, "n2"))
                A(rms, bank("n2")[:, 0:TT], ACT.Sqrt, scale=1.0 / D, bias=EPS).then_inc(*read("n2"))
                act.wait_ge(*at(l, "st_ckv", 16))
                for j in range(FFC):
                    act.wait_ge(*out(l, "fg", j))
                    if j >= 3:
                        act.wait_ge(*at(l, "ffn_conv", j - 2))
                        act.wait_ge(*at(l, "ffn_tail", j - 2))
                    copy(fc[:, j % 3, 2:258], bank("fg", j)[:, 0:TP])
                    copy(fs[:, j, 16:24], bank("fg", j)[:, TP:TT]).then_inc(*read("fg", j))
                    act.wait_ge(*at(l, "ffn_conv", j + 1))
                    if j >= 3:
                        act.wait_ge(*evac(l, "fu", j - 3))
                    A(fth[:, j % 3, :], fcv[:, j % 3, :], ACT.Tanh, scale=0.5).then_inc(*up("ffn_tanh"))
                act.wait_ge(*at(l, "ffn_sconv", 1))
                A(fts, fcs, ACT.Tanh, scale=0.5).then_inc(*up("ffn_stanh"))
                assert reads["A"] == len(READS["A"])
                close()
            act.wait_ge(read_by["V"], L * len(READS["V"]))
            A(xsq, x, ACT.Square).then_inc(last_squares, 1)
            act.wait_ge(last_sum, 1)
            A(rms, banks[:, 0, 0:TT], ACT.Sqrt, scale=1.0 / D, bias=EPS).then_inc(last_root, 1)

        @block.vector
        def _(dve):
            reads["V"] = 0
            V = nc.vector
            stt, tt_, ts = V.scalar_tensor_tensor, V.tensor_tensor, V.tensor_scalar
            dve.wait_ge(const_in, 16)
            dve.wait_ge(x_in, 16)
            dve.wait_ge(idx_ready, 16)
            ts(page_row[:], idx_raw[:], 8.0, const[:, C_PM:C_PM + 1], ALU.mult, ALU.add).then_inc(first_rows, 1)
            with dve.Fori(0, L) as l:
                link, close = stepper(dve, "dve", l)

                def normalise(name, g):
                    dve.wait_ge(*evac(l, name))
                    link(V.reciprocal(rms, rms))
                    for k in range(KT):
                        last = stt(hn[:, k, :], x[:, k, :], par[:, g + k:g + k + 1], rms, ALU.mult, ALU.mult)
                    last.then_inc(*up("hidden_norm"))

                dve.wait_ge(layer_open, l + 1)
                dve.wait_ge(*at(l, "par_loaded", 16))
                link(V.memset(ci[:, :, 24:27], 0.0))
                normalise("n1", Q_N1)

                dve.wait_ge(*out(l, "pS"))
                b = bank("pS")
                dve.wait_ge(*at(l, "beta_tanh", 1))
                ts(rt[:, 0, :], b[0:4, 0:TT], par[0:4, Q_ROW + 1:Q_ROW + 2], None, ALU.add)
                ts(rt[:, 1, :], b[96:100, 0:TT], par[0:4, Q_ROW + 3:Q_ROW + 4], -1.0, ALU.add, ALU.mult).then_inc(*up("row_x"))
                ts(rows[:, R_W, :], b[64:68, 0:TT], par[0:4, Q_ROW + 2:Q_ROW + 3], None, ALU.add).then_inc(*read("pS"))

                def rows_u():
                    dve.wait_ge(*at(l, "row_e", 1))
                    e, u, d = rt[:, 2:4, :], rt[:, 4:6, :], rt[:, 6:8, :]
                    ts(u, e, 1.0, None, ALU.add).then_inc(*up("row_u"))
                    dve.wait_ge(*at(l, "row_u", 1))
                    link(stt(d, u, -1.0, e, ALU.add, ALU.subtract))
                    link(V.reciprocal(e, u))
                    link(tt_(d, d, e, ALU.mult))
                    dve.wait_ge(*at(l, "beta_tanh", 1))
                    link(ts(rows[:, R_B, :], rows[:, R_B, :], 1.0, 0.5, ALU.add, ALU.mult))

                def rows_m():
                    dve.wait_ge(*at(l, "row_ln", 1))
                    dve.wait_ge(*at(l, "row_ea", 1))
                    ln = rows[:, R_M:R_M + 2, :]
                    xx, e, d = rt[:, 0:2, :], rt[:, 2:4, :], rt[:, 6:8, :]
                    link(stt(xx, xx, 0.0, ln, ALU.max, ALU.add))
                    link(tt_(xx, xx, d, ALU.subtract))
                    g, f, fs_ = rt[:, 0, :], rt[:, 1, :], rt[:, 2, :]
                    link(ts(g, g, ea, -1.0, ALU.mult, ALU.mult))
                    link(ts(f, f, -1.0, None, ALU.mult))
                    one = ones[0:4, :]
                    for c_ in range(NCH):
                        s = slice(c_ * P, (c_ + 1) * P)
                        V.tensor_tensor_scan(rows[:, R_G, s], one, g[:, s], 0.0, ALU.mult, ALU.add)
                        V.tensor_tensor_scan(fs_[:, s], one, f[:, s], 0.0, ALU.mult, ALU.add)
                    V.tensor_copy(rows[:, R_G, TP:TT], g[:, TP:TT])
                    link(V.tensor_copy(fs_[:, TP:TT], f[:, TP:TT]))
                    W, M = rows[:, R_W, :], rows[:, R_M, :]
                    link(tt_(W, W, fs_, ALU.subtract))
                    dve.wait_ge(*at(l, "m_loaded", 16))
                    link(V.tensor_tensor_scan(M[:, 0:P], W[:, 0:P], W[:, 0:P], 0.0, ALU.max, ALU.max))
                    link(tt_(mr[:, 0:P], M[:, 0:P], fs_[:, 0:P], ALU.add))
                    V.tensor_tensor_scan(M[:, P:TP], W[:, P:TP], W[:, P:TP], mr[:, P - 1:P], ALU.max, ALU.max)
                    link(tt_(M[:, TP:TT], W[:, TP:TT], m0s, ALU.max))
                    tt_(mr[:, P:TT], M[:, P:TT], fs_[:, P:TT], ALU.add).then_inc(*up("row_m"))
                    ts(nml, M[:, P - 1:TP:P], -1.0, None, ALU.mult)
                    tt_(rt[:, 3, 0:NB], m0s, M[:, TP:TT], ALU.subtract)
                    tt_(rt[:, 3, NB:2 * NB], W[:, TP:TT], M[:, TP:TT], ALU.subtract).then_inc(*up("row_m0"))

                for j in range(13):
                    if j < 12:
                        dve.wait_ge(*evac(l, "pq", j))
                        cv = cvr[:, j % 3, 0:TP]
                        w = [par[:, Q_CW + 4 * j + t:Q_CW + 4 * j + t + 1] for t in range(4)]
                        link(ts(cv, ci[:, j, 24:24 + TP], w[0], None, ALU.mult))
                        for t in (1, 2):
                            link(stt(cv, ci[:, j, 24 + t:24 + t + TP], w[t], cv, ALU.mult, ALU.add))
                        stt(cv, ci[:, j, 27:27 + TP], w[3], cv, ALU.mult, ALU.add).then_inc(*up("conv"))
                    if j >= 1:
                        dve.wait_ge(*at(l, "conv", j))
                        dve.wait_ge(*at(l, "conv_tanh", j))
                        stt(qkv[:, j - 1, 0:TP], thr[:, (j - 1) % 3, 0:TP], 1.0, cvr[:, (j - 1) % 3, 0:TP],
                            ALU.add, ALU.mult).then_inc(*up("silu"))
                    if j == 4:
                        rows_u()
                    if j == 7:
                        rows_m()
                dve.wait_ge(*at(l, "hist_loaded", 16))
                cw = par[:, Q_CW:Q_CW + 48].rearrange("p (j t) -> p j t", t=4)
                tmp = thr[:, 0, 0:96].rearrange("p (j n) -> p j n", j=12)
                for t in range(4):
                    src = ci[:, :, 8 * t:8 * t + 8] if t < 3 else ci[:, :, 27 + TP:27 + TT]
                    link(tt_(tmp if t else cvs, src, cw[:, :, t:t + 1].to_broadcast((P, 12, NB)), ALU.mult))
                    if t == 3:
                        tt_(cvs, cvs, tmp, ALU.add).then_inc(*up("sconv"))
                    elif t:
                        link(tt_(cvs, cvs, tmp, ALU.add))
                dve.wait_ge(*at(l, "sconv", 1))
                dve.wait_ge(*at(l, "sconv_tanh", 1))
                stt(qkv[:, 0:12, TP:TT], ths, 1.0, cvs, ALU.add, ALU.mult).then_inc(*up("silu"))
                for j in range(4):
                    dve.wait_ge(*at(l, "z_tanh", j + 1))
                    stt(z[:, j, :], z[:, j, :], 1.0, bank("pz", j)[:, 0:TT], ALU.add, ALU.mult).then_inc(*read("pz", j))
                dve.wait_ge(*at(l, "rows_act", 1))
                tt_(rows[:, R_BEG, :], rows[:, R_B, :], rows[:, R_EG, :], ALU.mult).then_inc(*up("rows_dve"))
                dve.wait_ge(*out(l, "rowT"))
                V.tensor_copy(cols, bank("rowT")[:, 0:48]).then_inc(*read("rowT"))
                for i in (0, 4):
                    dve.wait_ge(*evac(l, "l2", i + 3))
                    link(V.reciprocal(l2rt[:, i:i + 4, :], l2rt[:, i:i + 4, :]))
                    last = tt_(qkv[:, i:i + 4, :], qkv[:, i:i + 4, :], l2rt[:, i:i + 4, :], ALU.mult)
                last.then_inc(*up("qk_unit"))
                dve.wait_ge(*at(l, "qk_unit", 1))
                dve.wait_ge(*evac(l, "rowT"))
                dve.wait_ge(*at(l, "conv_state", 1))
                for h in range(NH):
                    b = bank("bcB", h)
                    dve.wait_ge(*out(l, "bcB", h))
                    tt_(qkv[:, 12 + h, 0:TP], qkv[:, 4 + h, 0:TP], b[:, 0:TP], ALU.mult)
                    V.tensor_copy(bes[:, h, :], b[:, TP:TT]).then_inc(*read("bcB", h))
                    b = bank("bcG", h)
                    dve.wait_ge(*out(l, "bcG", h))
                    ts(dec[:, h, :], b[:, 0:P], cols[:, h:h + 1], 0.0, ALU.subtract, ALU.min)
                    ts(dec[:, 4 + h, :], b[:, P:TP], cols[:, 24 + h:25 + h], 0.0, ALU.subtract, ALU.min).then_inc(*read("bcG", h))
                    b = bank("bcE", h)
                    dve.wait_ge(*out(l, "bcE", h))
                    tt_(qe[:, h, :], qkv[:, h, P:TP], b[:, P:TP], ALU.mult).then_inc(*up("decay_in"))
                    V.tensor_copy(egl[:, h, :], b[:, TP - 1:TT]).then_inc(*read("bcE", h))
                for c_ in range(NCH):
                    dve.wait_ge(*out(l, "vT", c_))
                    for h in range(NH):
                        k = (c_ * 6 + 1) * 4 + h
                        last = ts(bv[:, 4 * c_ + h, :], bank("vT", c_)[:, h * P:(h + 1) * P], cols[:, k:k + 1], 0.5, ALU.mult, ALU.mult)
                    last.then_inc(*read("vT", c_))
                dve.wait_ge(*at(l, "decay_masked", 1))
                for i in range(8):
                    dve.wait_ge(*out(l, "aq", i))
                    tt_(aq[:, i], heads(bank("aq", i)[:, 0:256], P), dec[:, i:i + 1, :].to_broadcast((P, 2, P)), ALU.mult).then_inc(*read("aq", i))
                for j in range(LEVELS):
                    for name, t in (("T", tm), ("TT", tt)):
                        if name == "T" and j == LEVELS - 1:
                            continue
                        for c_ in range(NCH):
                            i = 2 * j + c_
                            dst = t[:, 4 * c_:4 * c_ + 4, :]
                            old = ident.unsqueeze(1).to_broadcast((P, 4, P)) if j == 0 else dst
                            if j:
                                dve.wait_ge(*evac(l, name, i - 2))
                            dve.wait_ge(*out(l, name, i))
                            tt_(dst, old, heads(bank(name, i), P), ALU.subtract).then_inc(*read(name, i))
                dve.wait_ge(*out(l, "ks"))
                for h in range(NH):
                    k = (6 + 3) * 4 + h
                    last = stt(bv[:, h, :], bank("ks")[:, h * P:(h + 1) * P], cols[:, k:k + 1], bv[:, 4 + h, :], ALU.mult, ALU.subtract)
                last.then_inc(*read("ks"))
                dve.wait_ge(*out(l, "s2"))
                dve.wait_ge(*evac(l, "s1"))
                dve.wait_ge(*evac(l, "bcE", 3))
                for h in range(NH):
                    last = stt(s1[:, h, :], s1[:, h, :], egl[:, h, 0:1], bank("s2")[:, h * P:(h + 1) * P], ALU.mult, ALU.add)
                last.then_inc(*read("s2"))
                qk_, ks_, vns, oo, t1 = sm[0], sm[1], sm[2], sm[3], sm[4]
                egs = egl[:, :, 1:9]
                V.tensor_copy(ks_, qkv[:, 4:8, TP:TT])
                tt_(qk_, qkv[:, 0:4, TP:TT], qkv[:, 4:8, TP:TT], ALU.mult).then_inc(*up("sample_prods"))
                dve.wait_ge(*out(l, "sk"))
                kq = bank("sk")[:, 0:2 * NS].rearrange("p (h n t) -> p t h n", h=4, t=2)
                link(tt_(t1, egs, kq[:, 1], ALU.mult))
                link(stt(t1, qkv[:, 8:12, TP:TT], 0.5, t1, ALU.mult, ALU.subtract))
                tt_(vns, t1, bes, ALU.mult).then_inc(*up("sample_vnew"))
                tt_(oo, egs, kq[:, 0], ALU.mult).then_inc(*read("sk"))
                dve.wait_ge(*at(l, "sample_vnew", 1))
                dve.wait_ge(*out(l, "qk"))
                link(tt_(t1, vns, heads(bank("qk")[:, 0:NS], NB), ALU.mult))
                dve.wait_ge(*evac(l, "sk"))
                tt_(oa[:, :, TP:TT], oo, t1, ALU.add).then_inc(*read("qk"))
                dve.wait_ge(*at(l, "s_decayed", 1))
                for j in range(8):
                    dve.wait_ge(*out(l, "out", j))
                    tt_(S[:, 4 * j:4 * j + 4, :], S[:, 4 * j:4 * j + 4, :], heads(bank("out", j), P), ALU.add).then_inc(*read("out", j))
                dve.wait_ge(*evac(l, "na", 3))
                link(V.reciprocal(nrt, nrt))
                link(tt_(oa, oa, nrt, ALU.mult))
                stt(oa, oa, par[:, Q_GN:Q_GN + 1], z, ALU.mult, ALU.mult).then_inc(*up("oa_done"))
                dve.wait_ge(*out(l, "pa", 1))
                b = bank("pa", 1)
                r0, r1 = rot[64:96, 0:TT], rot[64:96, TT:2 * TT]
                tt_(r0, b[96:128, 0:TT], rope[96:128, :], ALU.mult)
                link(tt_(r1, b[64:96, 0:TT], rope[64:96, :], ALU.mult))
                tt_(kr[64:96, :], r0, r1, ALU.add).then_inc(*read("pa", 1))

                dve.wait_ge(*at(l, "oa_done", 1))
                dve.wait_ge(*at(l, "st_ps", 16))
                V.memset(vt[:, :, P:P + 1], 1.0).then_inc(*up("ones_column"))
                for h in range(NH):
                    b = bank("bcM", h)
                    dve.wait_ge(*out(l, "bcM", h))
                    ts(dm[:, h, :], b[:, 0:P], cols[:, 16 + h:17 + h], 0.0, ALU.subtract, ALU.max)
                    ts(dm[:, 4 + h, :], b[:, P:TP], cols[:, 40 + h:41 + h], 0.0, ALU.subtract, ALU.max).then_inc(*read("bcM", h))
                    b = bank("bcI", h)
                    dve.wait_ge(*out(l, "bcI", h))
                    dve.wait_ge(*evac(l, "pm", 1))
                    tt_(qs[:, h, :], mq[:, h, P:TP], b[0:64, P:TP], ALU.mult).then_inc(*up("mdecay_in"))
                    V.tensor_copy(ims[:, h, :], b[:, TP - 1:TT]).then_inc(*read("bcI", h))
                dve.wait_ge(*out(l, "bcW"))
                V.tensor_copy(wks, heads(bank("bcW")[:, 0:NS], NB)).then_inc(*read("bcW"))
                dve.wait_ge(*at(l, "mdecay_masked", 1))
                for c_ in range(NCH):
                    dve.wait_ge(*out(l, "mqk", c_))
                    tt_(pt[:, 4 * c_:4 * c_ + 4, :], dm[:, 4 * c_:4 * c_ + 4, :], heads(bank("mqk", c_), P), ALU.mult).then_inc(*read("mqk", c_))

                def divide(c_):
                    s = slice(c_ * P, (c_ + 1) * P)
                    dve.wait_ge(*evac(l, f"md{c_}"))
                    dve.wait_ge(*evac(l, "bcR", 3))
                    link(tt_(den, den, emr[:, :, s], ALU.max))
                    link(V.reciprocal(den, den))
                    dve.wait_ge(*out(l, f"mn{c_}"))
                    tt_(oc[:, :, s], den, heads(bank(f"mn{c_}"), P), ALU.mult).then_inc(*read(f"mn{c_}"))

                divide(0)
                divide(1)
                dve.wait_ge(*evac(l, "bcI", 3))
                for i in range(2):
                    dve.wait_ge(*out(l, "mc2", i))
                    for j in range(2):
                        h = 2 * i + j
                        last = stt(c1[:, h, :], c1[:, h, :], ims[0:64, h, 0:1], bank("mc2", i)[0:64, j * 129:(j + 1) * 129], ALU.mult, ALU.add)
                    last.then_inc(*read("mc2", i))
                im = ims[:, :, 1:9]
                n3 = mn.rearrange("p (h n) -> p h n", h=4)
                qn_, qk_, kw_, vs_, t0, t1, t2 = ms[0], ms[1], ms[2], ms[3], ms[4], ms[5], ms[6]
                dve.wait_ge(*at(l, "n_loaded", 16))
                dve.wait_ge(*evac(l, "bcW"))
                tt_(qn_[0:64], mq[:, :, TP:TT], n3, ALU.mult)
                tt_(qk_[0:64], mq[:, :, TP:TT], mk[:, :, TP:TT], ALU.mult).then_inc(*up("msample_prods"))
                V.tensor_copy(vs_, mv[:, :, TP:TT])
                tt_(kw_[0:64], mk[:, :, TP:TT], wks[0:64], ALU.mult).then_inc(*up("msample_kv"))
                dve.wait_ge(*out(l, "mq"))
                tt_(t0, im, heads(bank("mq")[:, 0:NS], NB), ALU.mult).then_inc(*read("mq"))
                dve.wait_ge(*out(l, "mqn"))
                b = bank("mqn")
                link(tt_(t1, wks, heads(b[:, NS:2 * NS], NB), ALU.mult))
                link(tt_(t2, im, heads(b[:, 0:NS], NB), ALU.mult))
                tt_(t2, t2, t1, ALU.add).then_inc(*read("mqn"))
                dve.wait_ge(*evac(l, "mqn"))
                link(tt_(t1, t1, vs_, ALU.mult))
                link(tt_(t0, t0, t1, ALU.add))
                link(stt(t2, t2, -1.0, t2, ALU.mult, ALU.max))
                link(tt_(t2, t2, emr[:, :, TP:TT], ALU.max))
                link(V.reciprocal(t2, t2))
                link(tt_(oc[:, :, TP:TT], t0, t2, ALU.mult))
                dve.wait_ge(*at(l, "msample_kv", 1))
                link(tt_(n3, n3, im[0:64], ALU.mult))
                tt_(n3, n3, kw_[0:64], ALU.add).then_inc(*up("n_new"))
                stt(oc, mo, 1.0, oc, ALU.add, ALU.mult).then_inc(*up("oc_raw"))
                dve.wait_ge(*at(l, "c_decayed", 1))
                for j in range(8):
                    dve.wait_ge(*out(l, "mout", j))
                    tt_(C[:, 4 * j:4 * j + 4, :], C[:, 4 * j:4 * j + 4, :], heads(bank("mout", j)[0:64], P), ALU.add).then_inc(*read("mout", j))
                dve.wait_ge(*evac(l, "nc", 3))
                link(V.reciprocal(crt, crt))
                stt(oc, oc, par[:, Q_MN:Q_MN + 1], crt, ALU.mult, ALU.mult).then_inc(*up("oc_done"))

                dve.wait_ge(*at(l, "oc_done", 1))
                dve.wait_ge(*at(l, "st_pc", 16))
                dve.wait_ge(*at(l, "st_sn", 16))
                dve.wait_ge(*at(l, "st_sc", 128))
                dve.wait_ge(*at(l, "st_conv", 16))
                dve.wait_ge(*evac(l, "nq"))
                link(V.reciprocal(art, art))
                stt(ckn, ckv, par[:, Q_KN:Q_KN + 1], art[:, 0, :], ALU.mult, ALU.mult).then_inc(*up("latent_out"))
                for k in range(2):
                    last = stt(cqn[:, k, :], cq[:, k, :], par[:, Q_QN + k:Q_QN + k + 1], art[:, 1, :], ALU.mult, ALU.mult)
                last.then_inc(*up("latent_norm"))
                dve.wait_ge(*evac(l, "pa", 1))
                V.tensor_copy(kf[64:96, :, :], kr[64:96, :].unsqueeze(1).to_broadcast((32, MH, TT))).then_inc(*up("key_copied"))
                for h in range(MH):
                    b = bank("uq", h)
                    dve.wait_ge(*out(l, "uq", h))
                    r0, r1 = rot[64:96, 0:TT], rot[64:96, TT:2 * TT]
                    tt_(r0, b[96:128, 0:TT], rope[96:128, :], ALU.mult)
                    link(tt_(r1, b[64:96, 0:TT], rope[64:96, :], ALU.mult))
                    link(tt_(qf[64:96, h, :], r0, r1, ALU.add))
                    V.tensor_copy(qf[0:64, h, :], b[0:64, 0:TT]).then_inc(*read("uq", h))
                for h in range(MH):
                    dve.wait_ge(*out(l, "sc", h))
                    tt_(ss[:, h, :], bank("sc", h)[:, 0:384], caus, ALU.add).then_inc(*read("sc", h))
                dve.wait_ge(*evac(l, "sc", 7))
                V.tensor_reduce(mx[:, 0, :], ss[:, :, 0:P], AX_X, ALU.max)
                link(V.tensor_reduce(mx[:, 1, :], ss[:, :, P:3 * P], AX_X, ALU.max))
                ts(nmx, mx, -SCALE, None, ALU.mult).then_inc(*up("neg_max"))
                dve.wait_ge(*evac(l, "ql"))
                tt_(pr1, ql, ckn[:, TP:TT].unsqueeze(1).to_broadcast((P, MH, NB)), ALU.mult)
                tt_(pr2[64:96], qf[64:96, :, TP:TT], kf[64:96, :, TP:TT], ALU.mult).then_inc(*up("new_prods"))
                link(V.memset(qrb, 0.0))
                for i in range(4):
                    last = V.tensor_copy(qrb[32 * i:32 * i + 32, :, i, :], qf[64:96, :, TP:TT].rearrange("p h n -> p n h"))
                last.then_inc(*up("query_blocks"))
                dve.wait_ge(*at(l, "probs_raw", 1))
                link(V.reciprocal(smm, smm))
                tt_(ss[:, :, 0:P], ss[:, :, 0:P], smm[:, 0, :].unsqueeze(2).to_broadcast((P, MH, P)), ALU.mult)
                tt_(ss[:, :, P:3 * P], ss[:, :, P:3 * P], smm[:, 1, :].unsqueeze(2).to_broadcast((P, MH, 2 * P)), ALU.mult).then_inc(*up("probs"))
                dve.wait_ge(*out(l, "sn"))
                V.tensor_copy(snew, heads(bank("sn")[:, 0:64], 8)).then_inc(*read("sn"))
                dve.wait_ge(*evac(l, "pv", 3))
                for n in range(NB + 1):
                    if n < NB:
                        if n > 0:
                            dve.wait_ge(*out(l, "ss", n - 1))
                        for q in (1, 3):
                            dve.wait_ge(*out(l, "ltr", 4 * n + q))
                            V.tensor_copy(ltt[:, 4 * q:4 * q + 4, :], heads(bank("ltr", 4 * n + q), P)).then_inc(*read("ltr", 4 * n + q))
                        dve.wait_ge(*out(l, "ss", n))
                        V.tensor_copy(ssb, heads(bank("ss", n)[:, 0:128], 8)).then_inc(*read("ss", n))
                        dve.wait_ge(*evac(l, "ss", n))
                        V.tensor_reduce(bm[:, n % 2, :], ssb.rearrange("p r h -> p h r"), AX_X, ALU.max).then_inc(*up("page_max"))
                    if n > 0:
                        m = (n - 1) % 2
                        dve.wait_ge(*at(l, "page_exp", n))
                        V.tensor_reduce(bs[:, m, :], pb[:, m].rearrange("p r h -> p h r"), AX_X, ALU.add).then_inc(*up("page_sums"))
                        dve.wait_ge(*out(l, "cs", n - 1))
                        b = bank("cs", n - 1)
                        link(tt_(rd[:, 0, :], pn[:, m, :], b[:, 8:16], ALU.add))
                        link(stt(rd[:, 1, :], pn[:, m, :], ckn[:, TP + n - 1:TP + n], b[:, 0:8], ALU.mult, ALU.add))
                        link(V.reciprocal(rd[:, 0, :], rd[:, 0, :]))
                        tt_(ctxs[:, :, n - 1], rd[:, 0, :], rd[:, 1, :], ALU.mult).then_inc(*read("cs", n - 1))
                    if n < NB:
                        dve.wait_ge(*out(l, "mxT", n))
                        V.tensor_reduce(mx8, bank("mxT", n)[0:8, 0:P], AX_X, ALU.max).then_inc(*read("mxT", n))
                        dve.wait_ge(*out(l, "mxB", n))
                        tt_(mxb[:, n % 2, :], snew[:, :, n], bank("mxB", n)[:, 0:8], ALU.max).then_inc(*read("mxB", n))
                        dve.wait_ge(*evac(l, "mxB", n))
                        top = mxb[:, n % 2, :]
                        tt_(pb[:, n % 2], ssb, top.unsqueeze(1).to_broadcast((P, NR, MH)), ALU.subtract)
                        tt_(pn[:, n % 2, :], snew[:, :, n], top, ALU.subtract).then_inc(*up("page_sub"))

                dve.wait_ge(*out(l, "ov"))
                for n in range(8):
                    for i in range(3):
                        k = 3 * n + i
                        dve.wait_ge(*evac(l, "pg", k))
                        dve.wait_ge(*out(l, "pb", k))
                        if i < 2:
                            stt(mg[:, n, :] if i == 0 else mt[:, 0, :], gt[:, k % 6, :], 1.0, bank("pb", k)[:, 0:TT],
                                ALU.add, ALU.mult).then_inc(*read("pb", k))
                        else:
                            dve.wait_ge(*evac(l, "pb", k - 1))
                            link(tt_(mg[:, n, :], mg[:, n, :], mt[:, 0, :], ALU.add))
                            stt(mt[:, 1, :], gt[:, k % 6, :], 1.0, bank("pb", k)[:, 0:TT], ALU.add, ALU.mult).then_inc(*read("pb", k))
                            dve.wait_ge(*evac(l, "pb", k))
                            tt_(mg[:, n, :], mg[:, n, :], mt[:, 1, :], ALU.add).then_inc(*up("merged"))
                for n in range(8):
                    dve.wait_ge(*out(l, "pw", n))
                    stt(x[:, n, :], bank("pw", n)[:, 0:TT], 0.5, x[:, n, :], ALU.mult, ALU.add).then_inc(*read("pw", n))
                dve.wait_ge(*at(l, "st_ckv", 16))
                V.memset(fc[:, :, 0:2], 0.0).then_inc(*up("ffn_zeros"))
                normalise("n2", Q_N2)

                dve.wait_ge(*at(l, "ffn_zeros", 1))
                for j in range(FFC):
                    w = [par[:, Q_FW + 3 * j + t:Q_FW + 3 * j + t + 1] for t in range(3)]
                    cv = fcv[:, j % 3, :]
                    dve.wait_ge(*evac(l, "fg", j))
                    link(ts(cv, fc[:, j % 3, 0:TP], w[0], par[:, Q_FB + j:Q_FB + j + 1], ALU.mult, ALU.add))
                    link(stt(cv, fc[:, j % 3, 1:1 + TP], w[1], cv, ALU.mult, ALU.add))
                    stt(cv, fc[:, j % 3, 2:2 + TP], w[2], cv, ALU.mult, ALU.add).then_inc(*up("ffn_conv"))
                    dve.wait_ge(*at(l, "ffn_conv", j + 1))
                    dve.wait_ge(*at(l, "ffn_tanh", j + 1))
                    link(stt(cv, fth[:, j % 3, :], 1.0, cv, ALU.add, ALU.mult))
                    dve.wait_ge(*out(l, "fu", j))
                    tt_(hid[:, j, 0:TP], cv, bank("fu", j)[:, 0:TP], ALU.mult)
                    V.tensor_copy(us[:, j, :], bank("fu", j)[:, TP:TT]).then_inc(*read("fu", j))
                dve.wait_ge(*at(l, "fh_loaded", 16))
                dve.wait_ge(*evac(l, "fu", FFC - 1))
                fw = par[:, Q_FW:Q_FW + 66].rearrange("p (j t) -> p j t", t=3)
                wide = (P, FFC, NB)
                link(tt_(fcs, fs[:, :, 0:8], fw[:, :, 0:1].to_broadcast(wide), ALU.mult))
                link(tt_(fcs, fcs, par[:, Q_FB:Q_FB + FFC].unsqueeze(2).to_broadcast(wide), ALU.add))
                link(tt_(fts, fs[:, :, 8:16], fw[:, :, 1:2].to_broadcast(wide), ALU.mult))
                link(tt_(fcs, fcs, fts, ALU.add))
                link(tt_(fts, fs[:, :, 16:24], fw[:, :, 2:3].to_broadcast(wide), ALU.mult))
                tt_(fcs, fcs, fts, ALU.add).then_inc(*up("ffn_sconv"))
                dve.wait_ge(*at(l, "ffn_sconv", 1))
                dve.wait_ge(*at(l, "ffn_stanh", 1))
                link(stt(fcs, fts, 1.0, fcs, ALU.add, ALU.mult))
                tt_(hid[:, :, TP:TT], fcs, us, ALU.mult).then_inc(*up("hidden"))
                for i in range(2):
                    dve.wait_ge(*at(l, f"lat_in{i}", 32 * NB // 2))
                ts(page_row[:], page_row[:], float(NPOOL * 8), None, ALU.add).then_inc(*up("next_rows"))
                for n in range(8):
                    dve.wait_ge(*out(l, "fd", n))
                    stt(x[:, n, :], bank("fd", n)[:, 0:TT], 0.5, x[:, n, :], ALU.mult, ALU.add).then_inc(*read("fd", n))
                assert reads["V"] == len(READS["V"])
                close()
            dve.wait_ge(last_root, 1)
            V.reciprocal(rms, rms).then_inc(last_norm, 1)
            dve.wait_ge(last_norm, 1)
            for k in range(KT):
                last = stt(hn[:, k, :], x[:, k, :], par[:, Q_NF + k:Q_NF + k + 1], rms, ALU.mult, ALU.mult)
            last.then_inc(last_norm, 1)

        @block.gpsimd
        def _(pool):
            dma = nc.gpsimd.dma_start
            tt_ = nc.gpsimd.tensor_tensor
            dma(const, a["const"]).then_inc(const_in, 16)
            dma(x.rearrange("p k n -> p (k n)"), a["x"]).then_inc(x_in, 16)
            dma(idx_raw[:], a["pages"]).then_inc(idx_ready, 16)

            def plain():
                pool.sem_inc(spare["pool"], 1)

            def row(name, l):
                return a[name][bass.ds(l, 1)].rearrange("a p n -> p (a n)")

            pool.sem_inc(layer_open, 1)
            with pool.Fori(0, L) as l:
                link, close = stepper(pool, "pool", l)
                pool.wait_ge(layer_open, l + 1)
                plain()
                dma(par, row("par", l)).then_inc(*up("par_loaded", 16))
                dma(m0s, row("m0", l)).then_inc(*up("m_loaded", 16))
                dma(ci[:, :, 0:24], a["conv0"][bass.ds(l, 1)].rearrange("a p (j n) -> p (a j) n", j=12)).then_inc(*up("hist_loaded", 16))
                dma(S.rearrange("p s n -> p (s n)"), row("s0", l)).then_inc(*up("s_loaded", 16))
                pool.wait_ge(*evac(l, "pq", 11))
                pool.wait_ge(*at(l, "hist_loaded", 16))
                plain()
                nc.gpsimd.tensor_copy(co[:, :, 0:3], ci[:, :, 24 + TP:27 + TP])
                nc.gpsimd.tensor_copy(co[:, :, 3:19], ci[:, :, 8:24])
                nc.gpsimd.tensor_copy(co[:, :, 19:27], ci[:, :, 27 + TP:27 + TT]).then_inc(*up("conv_state"))
                pool.wait_ge(*at(l, "conv_state", 1))
                plain()
                dma(row("conv_o", l), co.rearrange("p j n -> p (j n)")).then_inc(*up("st_conv", 16))
                pool.wait_ge(*at(l, "row_m0", 1))
                plain()
                dma(row("m_o", l), mr[:, TP - 1:TT]).then_inc(*up("st_m", 16))
                pool.wait_ge(*at(l, "decay_exp", 1))
                tt_(dec, dec, inc_mask.unsqueeze(1).to_broadcast((P, 8, P)), ALU.mult).then_inc(*up("decay_masked"))
                for j in range(LEVELS):
                    for c_ in range(NCH):
                        if j == 0:
                            pool.wait_ge(*evac(l, "aq", 4 * c_ + 3))
                        else:
                            pool.wait_ge(*out(l, "Y", 2 * j - 2 + c_))
                        lvl = const[:, C_LVL + j * P:C_LVL + (j + 1) * P].unsqueeze(1).to_broadcast((P, 4, P))
                        tt_(am[:, c_], aq[:, 4 * c_:4 * c_ + 4, 1, :], lvl, ALU.mult).then_inc(*up("level_a"))
                pool.wait_ge(*evac(l, "s2"))
                plain()
                dma(row("ps_o", l), s1.rearrange("p h n -> p (h n)")).then_inc(*up("st_ps", 16))
                pool.wait_ge(*out(l, "sk"))
                pool.wait_ge(*evac(l, "bcE", 3))

                def update(st, n, name_t, name_o, ready, dst):
                    for j in range(8):
                        if j == 0:
                            pool.wait_ge(*evac(l, name_t))
                        if j >= 2:
                            pool.wait_ge(*out(l, name_o, j - 2))
                        tt_(vd[:, j % 2], kvt[:, P:2 * P].unsqueeze(1).to_broadcast((NS, 4, P)),
                            ident[0:NS, 4 * j:4 * j + 4].unsqueeze(2).to_broadcast((NS, 4, P)), ALU.mult).then_inc(*up(ready))
                    for j in range(8):
                        pool.wait_ge(*evac(l, name_o, j))
                        plain()
                        dma(a[dst][bass.ds(l, 1), :, 512 * j:512 * (j + 1)].rearrange("a p n -> p (a n)"),
                            st[:, 4 * j:4 * j + 4, :].rearrange("p s n -> p (s n)")).then_inc(*up("st_" + n, 16))

                tt_(S.rearrange("p (h n) v -> p h n v", h=4), S.rearrange("p (h n) v -> p h n v", h=4),
                    egl[:, :, 1:9].unsqueeze(3).to_broadcast((P, 4, NB, P)), ALU.mult).then_inc(*up("s_decayed"))
                update(S, "ss", "kvT", "out", "v_diag", "ss_o")
                pool.wait_ge(*at(l, "st_ss", 128))
                plain()
                dma(C.rearrange("p s n -> p (s n)"), row("c0", l)).then_inc(*up("c_loaded", 16))
                pool.wait_ge(*at(l, "oa_done", 1))
                pool.wait_ge(*at(l, "st_ps", 16))
                plain()
                dma(mn, row("n0", l)).then_inc(*up("n_loaded", 16))
                pool.wait_ge(*at(l, "mdecay_exp", 1))
                tt_(dm, dm, inc_mask.unsqueeze(1).to_broadcast((P, 8, P)), ALU.mult).then_inc(*up("mdecay_masked"))
                pool.wait_ge(*evac(l, "mc2", 1))
                plain()
                dma(row("pc_o", l), c1.rearrange("p h n -> p (h n)")).then_inc(*up("st_pc", 16))
                pool.wait_ge(*at(l, "n_new", 1))
                plain()
                dma(row("sn_o", l), mn).then_inc(*up("st_sn", 16))
                pool.wait_ge(*out(l, "mq"))
                pool.wait_ge(*evac(l, "bcI", 3))
                tt_(C.rearrange("p (h n) v -> p h n v", h=4), C.rearrange("p (h n) v -> p h n v", h=4),
                    ims[0:64, :, 1:9].unsqueeze(3).to_broadcast((64, 4, NB, P)), ALU.mult).then_inc(*up("c_decayed"))
                update(C, "sc", "mkvT", "mout", "mv_diag", "sc_o")
                pool.wait_ge(*at(l, "oc_done", 1))
                pool.wait_ge(*at(l, "st_pc", 16))
                pool.wait_ge(*at(l, "st_sn", 16))
                pool.wait_ge(*at(l, "st_sc", 128))
                pool.wait_ge(*at(l, "st_conv", 16))
                plain()
                dma(arena[:, g0:g0 + 4096], row("mla_w", l)).then_inc(*up("mla_loaded", 16))
                pool.wait_ge(*at(l, "latent_out", 1))
                plain()
                dma(row("ckv_o", l), ckn).then_inc(*up("st_ckv", 16))
                pool.wait_ge(*evac(l, "pa", 1))
                plain()
                dma(row("kr_o", l), kr[64:96, :]).then_inc(*up("st_kr", 16))
                pool.wait_ge(*evac(l, "pv", 3))
                pool.wait_ge(first_rows, 1)
                plain()
                for n in range(NB):
                    if n >= 2:
                        pool.wait_ge(*out(l, "cs", n - 2))
                        plain()
                    for t, (dst, src) in enumerate(((lat[:, n % 2, 0:2048], a["lat"]), (lat[:, n % 2, 2048:2560], a["key"]))):
                        nc.gpsimd.indirect_dma_start(dst, None, src, bass.IndirectOffsetOnAxis(page_row[:, n:n + 1], 0)).then_inc(
                            *up(f"lat_in{n % 2}", 16))
                pool.wait_ge(*evac(l, "ov"))
                pool.wait_ge(*at(l, "st_ckv", 16))
                plain()
                dma(fs[:, :, 0:16], a["ffn0"][bass.ds(l, 1)].rearrange("a p (j n) -> p (a j) n", j=FFC)).then_inc(*up("fh_loaded", 16))
                for j in range(FFC):
                    pool.wait_ge(*evac(l, "fg", j))
                    plain()
                    nc.gpsimd.tensor_copy(fo[:, j, 0:2], fc[:, j % 3, 256:258]).then_inc(*up("ffn_tail"))
                pool.wait_ge(*at(l, "fh_loaded", 16))
                pool.wait_ge(*at(l, "ffn_tail", FFC))
                plain()
                link(nc.gpsimd.tensor_copy(fo[:, :, 2:18], fs[:, :, 8:24]))
                dma(row("ffn_o", l), fo.rearrange("p j n -> p (j n)")).then_inc(*up("st_ffn", 16))
                pool.wait_ge(*evac(l, "fd", 7))
                pool.wait_ge(*at(l, "next_rows", 1))
                for name in SIGNALS:
                    if name.startswith("st_"):
                        pool.wait_ge(*at(l, name, SIGNALS[name]))
                pool.sem_inc(layer_open, 1)
                close()
            pool.wait_ge(last_norm, 2)
            dma(a["y"], hn.rearrange("p k n -> p (k n)")).then_inc(y_out, 16)
            pool.wait_ge(y_out, 16)
        assert not [n for n in SIGNALS if given[n] != SIGNALS[n]], given


def tiles(w):
    k, n = w.shape
    return w.reshape(k // P, P, n // P, P).transpose(2, 1, 0, 3)


def stream(parts):
    flat = np.concatenate([t.transpose(0, 2, 1, 3).reshape(-1, P, P) for t in parts])
    return flat.reshape(-1, 8, P, P).transpose(0, 2, 1, 3).reshape(-1, P, 1024)


def layer_stream(w_in, wa, wb, wc, w_out, w_up, w_down):
    cut = np.split(w_in, np.cumsum([1536, 4, 4, 512, 256, 128, 32, 1024, 4, 4, 512]).tolist(), axis=1)
    qkv, beta, alpha, zz, cq, ckv, kr, ml, ci, cf, co, gates = cut
    pad = np.zeros((D, 28), w_in.dtype)
    small = np.concatenate([alpha, pad, beta, pad, ci, pad, cf, pad], axis=1)
    key = np.concatenate([np.zeros((D, 64), w_in.dtype), kr, kr[:, 16:], kr[:, :16]], axis=1)
    before = [small, qkv, zz]
    fills = [ml, co, ckv, key, cq]
    parts = [tiles(w) for w in before + fills]
    gt = tiles(gates).reshape(3, 8, P, KT, P)
    br = [tiles(w) for w in (wa, wb, wc)]
    for n in range(8):
        parts += [gt[:, n]] + [b[n:n + 1] for b in br]
    parts.append(tiles(w_out))
    up = tiles(w_up)
    parts.append(np.stack([up[FFC:], up[:FFC]], axis=1).reshape(2 * FFC, P, KT, P))
    parts.append(tiles(w_down))
    return stream(parts)


def chan(v, k):
    v = v.reshape(v.shape[:-1] + (k, P))
    return np.moveaxis(np.moveaxis(v, -1, 0), -1, 1)


def constants():
    i = np.arange(P)
    c = np.zeros((P, N_CONST), np.float32)
    c[:, C_ID:C_ID + P] = np.eye(P)
    c[:, C_ONE:C_ONE + P] = 1.0
    c[:, C_INC:C_INC + P] = i[:, None] <= i[None, :]
    for j in range(LEVELS):
        same = (i[:, None] >> (j + 1)) == (i[None, :] >> (j + 1))
        c[:, C_LVL + j * P:C_LVL + (j + 1) * P] = same & ((i[:, None] >> j) % 2 == 0) & ((i[None, :] >> j) % 2 == 1)
    later = np.where(i[None, :] > i[:, None], -1e30, 0.0)
    c[:, C_CAUS:C_CAUS + P] = later
    c[:, C_CAUS + 256:C_CAUS + 384] = later
    inv = (np.float32(10000.0) ** (-np.arange(16, dtype=np.float32) / np.float32(16))).astype(np.float32)
    pos = np.concatenate([np.arange(TP), np.full(NB, PAST)]).astype(np.float32)
    ang = (inv[:, None] * pos[None, :]).astype(np.float32).astype(np.float64)
    c[64:96, C_ROPE:C_ROPE + TT] = np.concatenate([np.cos(ang), np.cos(ang)])
    c[96:128, C_ROPE:C_ROPE + TT] = np.concatenate([-np.sin(ang), np.sin(ang)])
    c[:, C_PM] = i % 8
    return c


def kernel(**inputs):
    import concourse.bacc as bacc
    from concourse.bass_utils import run_bass_kernel_spmd as run

    w = {k: np.asarray(v) for k, v in inputs.items()}
    f32 = np.float32
    arrays = {}
    tok = np.concatenate([w["x_prompt"][0], w["x_sample"][:, 0]])
    arrays["x"] = chan(tok, KT).reshape(P, KT * TT)
    arrays["weights"] = np.concatenate([
        layer_stream(*(w[n][l] for n in ("w_in", "w_branch_a", "w_branch_b", "w_branch_c", "w_out", "ffn_w_up", "ffn_w_down")))
        for l in range(L)])
    arrays["const"] = constants()
    par = np.zeros((L, P, N_PAR), f32)
    mla = np.zeros((L, P, 4096), f32)
    for l in range(L):
        par[l, :, Q_N1:Q_N1 + 8] = chan(w["norm1_g"][l], 8)
        par[l, :, Q_N2:Q_N2 + 8] = chan(w["norm2_g"][l], 8)
        par[l, :, Q_CW:Q_CW + 48] = chan(w["gdn_conv_w"][l], 12).reshape(P, 48)
        par[l, :, Q_GN] = w["gdn_norm_g"][l]
        par[l, :, Q_QN:Q_QN + 2] = chan(w["mla_q_norm_g"][l], 2)
        par[l, :, Q_KN] = w["mla_kv_norm_g"][l]
        par[l, :, Q_MN] = w["ml_norm_g"][l]
        par[l, :, Q_FW:Q_FW + 66] = chan(w["ffn_conv_w"][l], FFC).reshape(P, 66)
        par[l, :, Q_FB:Q_FB + 22] = chan(w["ffn_conv_b"][l], FFC)
        par[l, :, Q_NF:Q_NF + 8] = chan(w["final_norm_g"], 8)
        for k, n in enumerate(("gdn_A_log", "gdn_dt_bias", "ml_b_i", "ml_b_f")):
            par[l, 0:4, Q_ROW + k] = w[n][l]
        uq = w["mla_w_uq"][l].reshape(2, P, 8, 96).transpose(1, 0, 2, 3)
        uq = np.concatenate([uq, uq[..., 80:96], uq[..., 64:80]], axis=-1)
        mla[l, :, 0:2048] = uq.reshape(P, 2048)
        mla[l, :, 2048:2560] = w["mla_w_uk"][l]
        mla[l, 0:64, 2560:3584] = w["mla_w_uk"][l].reshape(P, 8, 64).transpose(2, 1, 0).reshape(64, 1024)
        mla[l, :, 3584:4096] = w["mla_w_uv"][l]
    arrays["par"], arrays["mla_w"] = par, mla
    arrays["lat"] = w["cache_kv_latent"].reshape(L * NPOOL * 8, NR * 128)
    arrays["key"] = w["cache_k_rope"].reshape(L * NPOOL * 8, NR * 32)
    arrays["pages"] = np.repeat(np.ascontiguousarray(w["page_table"].T), 8, axis=0).astype(np.int32)
    arrays["conv0"] = w["state_gdn_conv"].transpose(0, 3, 2, 1).reshape(L, 12, P, 24).transpose(0, 2, 1, 3).reshape(L, P, 288)
    arrays["s0"] = w["state_gdn_S"].transpose(0, 3, 2, 1, 4).reshape(L, P, NS * 128)
    arrays["c0"] = w["state_mlstm_C"].transpose(0, 3, 2, 1, 4).reshape(L, 64, NS * 128)
    arrays["n0"] = w["state_mlstm_n"].transpose(0, 3, 2, 1).reshape(L, 64, NS)
    arrays["m0"] = w["state_mlstm_m"].transpose(0, 2, 1).reshape(L, 4, NB)
    arrays["ffn0"] = w["state_ffn_conv"].transpose(0, 3, 2, 1).reshape(L, FFC, P, 16).transpose(0, 2, 1, 3).reshape(L, P, FFC * 16)
    arrays = {k: np.ascontiguousarray(v) for k, v in arrays.items()}
    outs = dict(y=(P, KT * TT), ckv_o=(L, P, TT), kr_o=(L, 32, TT), conv_o=(L, P, 12 * 27), ps_o=(L, P, 512),
                ss_o=(L, P, NS * 128), pc_o=(L, 64, 516), sc_o=(L, 64, NS * 128), sn_o=(L, 64, NS),
                m_o=(L, 4, 9), ffn_o=(L, P, FFC * 18))
    nc = bacc.Bacc("TRN2", target_bir_lowering=False, num_devices=1)
    aps = {}
    for k, v in arrays.items():
        aps[k] = nc.dram_tensor("in_" + k, v.shape, mybir.dt.from_np(v.dtype), kind="ExternalInput").ap()
    for k, s in outs.items():
        aps[k] = nc.dram_tensor("out_" + k, s, F32, kind="ExternalOutput").ap()
    build(nc, aps)
    res = run(nc, [{"in_" + k: v for k, v in arrays.items()}], core_ids=[0]).results[0]
    g = {k: np.asarray(res["out_" + k]) for k in outs}

    y = g["y"].reshape(P, KT, TT).transpose(2, 1, 0).reshape(TT, D)
    ckv, kr = g["ckv_o"].transpose(0, 2, 1), g["kr_o"].transpose(0, 2, 1)
    cv = g["conv_o"].reshape(L, P, 12, 27).transpose(0, 3, 2, 1).reshape(L, 27, 1536)
    fo = g["ffn_o"].reshape(L, P, FFC, 18).transpose(0, 3, 2, 1).reshape(L, 18, FFC * P)
    pc = g["pc_o"].reshape(L, 64, 4, 129).transpose(0, 2, 1, 3)
    m = g["m_o"]
    out = (
        y[None, :TP], y[TP:, None],
        ckv[:, None, :TP], kr[:, None, :TP], cv[:, None, 0:3],
        g["ps_o"].reshape(L, P, 4, 128).transpose(0, 2, 1, 3)[:, None],
        pc[:, None, :, :, 0:128], pc[:, None, :, :, 128], m[:, None, :, 0], fo[:, None, 0:2],
        ckv[:, TP:, None], kr[:, TP:, None],
        cv[:, 3:].reshape(L, 3, NB, 1536).transpose(0, 2, 1, 3),
        g["ss_o"].reshape(L, P, 4, NB, 128).transpose(0, 3, 2, 1, 4),
        g["sc_o"].reshape(L, 64, 4, NB, 128).transpose(0, 3, 2, 1, 4),
        g["sn_o"].reshape(L, 64, 4, NB).transpose(0, 3, 2, 1),
        m[:, :, 1:].transpose(0, 2, 1),
        fo[:, 2:].reshape(L, 2, NB, FFC * P).transpose(0, 2, 1, 3),
    )
    return tuple(np.ascontiguousarray(v) for v in out)
```
